# Optimizing a Trainium2 kernel written in Bass

```python
import jax
import jax.numpy as jnp
from jax import lax
import numpy as np

D_MODEL = 1024
BATCH = 1
SEQ = 512
DEPTH = 2

N_MIXERS = 2
N_ATTN_LAYERS = (DEPTH + 1) // 2
N_RWKV_LAYERS = DEPTH // 2
HEAD_DIM = 64
N_HEADS = D_MODEL // HEAD_DIM
N_META = 16
BLOCK = 128
D_FF = ((-(-8 * D_MODEL // 3)) + 255) // 256 * 256
DECAY_LORA = max(32, int(round(1.8 * D_MODEL ** 0.5 / 32)) * 32)
AAA_LORA = max(32, int(round(1.8 * D_MODEL ** 0.5 / 32)) * 32)
MV_LORA = max(32, int(round(1.3 * D_MODEL ** 0.5 / 32)) * 32)
GATE_LORA = max(32, int(round(0.6 * D_MODEL ** 0.8 / 32)) * 32)
RMS_EPS = 1e-6
GN_EPS = 64e-5
L2_EPS = 1e-12

kernel_name = 'hybrid_stickbreak_rwkv7_block'

def rms_norm(x, g):
    xf = x.astype(jnp.float32)
    y = xf * lax.rsqrt(jnp.mean(xf * xf, axis=-1, keepdims=True) + RMS_EPS)
    return (y * g.astype(jnp.float32)).astype(x.dtype)

def swiglu(h, w_in, w_out):
    gate, up = jnp.split(jnp.einsum('btd,df->btf', h, w_in), 2, axis=-1)
    return jnp.einsum('btf,fd->btd', jax.nn.silu(gate) * up, w_out)

def stick_breaking_attention(h, w_qkv, w_o):
    B, T, D = h.shape
    q, k, v = jnp.split(jnp.einsum('btd,de->bte', h, w_qkv), 3, axis=-1)
    pad = (-N_META) % BLOCK
    tail = (-(T + pad)) % BLOCK
    Tp = T + pad + tail

    def heads(u):
        u = u.reshape(B, T, N_HEADS, HEAD_DIM).transpose(0, 2, 1, 3)
        return jnp.pad(u, ((0, 0), (0, 0), (pad, tail), (0, 0)))

    qh, kh, vh = heads(q), heads(k), heads(v)
    scale = HEAD_DIM ** -0.5
    outs = []
    for blk in range(Tp // BLOCK):
        L = (blk + 1) * BLOCK
        qb = qh[:, :, blk * BLOCK:L]
        kb = kh[:, :, :L]
        vb = vh[:, :, :L]
        z = jnp.einsum('bhtd,bhsd->bhts', qb, kb).astype(jnp.float32) * scale
        t_idx = blk * BLOCK + jnp.arange(BLOCK)
        s_idx = jnp.arange(L)
        mask = (s_idx[None, :] < t_idx[:, None]) & (s_idx[None, :] >= pad)
        log_beta = jax.nn.log_sigmoid(z)
        log_rest = jnp.where(mask, jax.nn.log_sigmoid(-z), 0.0)
        later = lax.cumsum(log_rest, axis=3, reverse=True) - log_rest
        att = jnp.where(mask, jnp.exp(log_beta + later), 0.0)
        outs.append(jnp.einsum('bhts,bhsd->bhtd', att.astype(vb.dtype), vb))
    o = jnp.concatenate(outs, axis=2)[:, :, pad:pad + T]
    o = o.transpose(0, 2, 1, 3).reshape(B, T, D)
    return jnp.einsum('btd,de->bte', o, w_o), v

def rwkv7_time_mix(h, v_first, mu, w_rkv, w_o, w0, w1, w2, a0, a1, a2, v0, v1, v2,
                   g1, g2, k_k, k_a, r_k, ln_x_w, ln_x_b):
    B, T, D = h.shape
    xx = jnp.pad(h, ((0, 0), (1, 0), (0, 0)))[:, :-1] - h
    xs = h[None] + xx[None] * mu[:, None, None, :]
    rkv = jnp.einsum('nbtd,nde->nbte', xs[:3], w_rkv)
    r, k, v = rkv[0], rkv[1], rkv[2]
    xv, xw, xa, xg = xs[2], xs[3], xs[4], xs[5]
    w_log = -jax.nn.softplus(-(w0 + jnp.einsum('btl,ld->btd', jnp.tanh(xw @ w1), w2)).astype(jnp.float32)) - 0.5
    decay = jnp.exp(-jnp.exp(w_log))
    v = v + (v_first - v) * jax.nn.sigmoid(v0 + (xv @ v1) @ v2)
    a = jax.nn.sigmoid(a0 + (xa @ a1) @ a2)
    g = jax.nn.sigmoid(xg @ g1) @ g2

    def hs(u):
        return u.astype(jnp.float32).reshape(B, T, N_HEADS, HEAD_DIM)

    kk = hs(k * k_k)
    kk = kk / jnp.maximum(jnp.sqrt(jnp.sum(kk * kk, axis=-1, keepdims=True)), L2_EPS)
    k = k * (1.0 + (a - 1.0) * k_a)
    r_h, k_h, v_h, a_h, w_h = hs(r), hs(k), hs(v), hs(a), hs(decay)

    def step(S, inp):
        r_t, w_t, k_t, v_t, a_t, b_t = inp
        sa = jnp.einsum('bhij,bhj->bhi', S, a_t)
        S = (S * w_t[:, :, None, :] + sa[..., None] * b_t[:, :, None, :]
             + v_t[..., None] * k_t[:, :, None, :])
        return S, jnp.einsum('bhij,bhj->bhi', S, r_t)

    seq_in = tuple(u.transpose(1, 0, 2, 3) for u in (r_h, w_h, k_h, v_h, -kk, kk * a_h))
    S0 = jnp.zeros((B, N_HEADS, HEAD_DIM, HEAD_DIM), jnp.float32)
    _, y = lax.scan(step, S0, seq_in)
    y = y.transpose(1, 0, 2, 3)
    mean = jnp.mean(y, axis=-1, keepdims=True)
    var = jnp.mean(jnp.square(y - mean), axis=-1, keepdims=True)
    y = ((y - mean) * lax.rsqrt(var + GN_EPS) * ln_x_w.astype(jnp.float32).reshape(N_HEADS, HEAD_DIM)
         + ln_x_b.astype(jnp.float32).reshape(N_HEADS, HEAD_DIM))
    bonus = jnp.sum(r_h * k_h * r_k.astype(jnp.float32), axis=-1, keepdims=True) * v_h
    y = (y + bonus).reshape(B, T, D).astype(h.dtype)
    return jnp.einsum('btd,de->bte', y * g, w_o)

def setup_inputs(seed: int = 0) -> dict:
    key = jax.random.key(seed)
    ks = jax.random.split(key, 32)
    D, H, N, F = D_MODEL, N_HEADS, HEAD_DIM, D_FF
    NA, NR = N_ATTN_LAYERS, N_RWKV_LAYERS

    def nrm(k, shape, scale):
        return jax.random.normal(k, shape, jnp.float32) * scale

    return {
        'x': nrm(ks[0], (BATCH, SEQ, D), 1.0),
        'meta_tokens': nrm(ks[1], (N_META, D), 1.0),
        'attn_norm': 1.0 + nrm(ks[2], (NA, D), 0.05),
        'w_qkv': nrm(ks[3], (NA, D, 3 * D), D ** -0.5),
        'w_o_attn': nrm(ks[4], (NA, D, D), D ** -0.5),
        'rwkv_norm': 1.0 + nrm(ks[5], (NR, D), 0.05),
        'rwkv_mu': jax.random.uniform(ks[6], (NR, 6, D), jnp.float32),
        'w_rkv': nrm(ks[7], (NR, 3, D, D), D ** -0.5),
        'w_o_rwkv': nrm(ks[8], (NR, D, D), D ** -0.5),
        'w0': jax.random.uniform(ks[9], (NR, D), jnp.float32, minval=-6.5, maxval=-1.5),
        'w1': nrm(ks[10], (NR, D, DECAY_LORA), D ** -0.5),
        'w2': nrm(ks[11], (NR, DECAY_LORA, D), DECAY_LORA ** -0.5),
        'a0': nrm(ks[12], (NR, D), 0.1),
        'a1': nrm(ks[13], (NR, D, AAA_LORA), D ** -0.5),
        'a2': nrm(ks[14], (NR, AAA_LORA, D), AAA_LORA ** -0.5),
        'v0': 1.0 + nrm(ks[15], (NR, D), 0.1),
        'v1': nrm(ks[16], (NR, D, MV_LORA), D ** -0.5),
        'v2': nrm(ks[17], (NR, MV_LORA, D), MV_LORA ** -0.5),
        'g1': nrm(ks[18], (NR, D, GATE_LORA), D ** -0.5),
        'g2': nrm(ks[19], (NR, GATE_LORA, D), GATE_LORA ** -0.5),
        'k_k': 0.85 + nrm(ks[20], (NR, D), 0.05),
        'k_a': 1.0 + nrm(ks[21], (NR, D), 0.05),
        'r_k': nrm(ks[22], (NR, H, N), 0.1),
        'ln_x_w': 1.0 + nrm(ks[23], (NR, D), 0.05),
        'ln_x_b': nrm(ks[24], (NR, D), 0.01),
        'ffn_norm': 1.0 + nrm(ks[25], (DEPTH, D), 0.05),
        'w_ffn_in': nrm(ks[26], (DEPTH, D, 2 * F), D ** -0.5),
        'w_ffn_out': nrm(ks[27], (DEPTH, F, D), F ** -0.5),
        'final_norm': 1.0 + nrm(ks[28], (D,), 0.05),
    }

def reference(x, meta_tokens, attn_norm, w_qkv, w_o_attn, rwkv_norm, rwkv_mu, w_rkv, w_o_rwkv,
              w0, w1, w2, a0, a1, a2, v0, v1, v2, g1, g2, k_k, k_a, r_k, ln_x_w, ln_x_b,
              ffn_norm, w_ffn_in, w_ffn_out, final_norm):
    B = x.shape[0]
    meta = jnp.broadcast_to(meta_tokens[None].astype(x.dtype), (B, N_META, D_MODEL))
    h = jnp.concatenate([meta, x], axis=1)
    v_first = None
    for i in range(DEPTH):
        j = i // N_MIXERS
        if i % N_MIXERS == 0:
            mix, v_layer = stick_breaking_attention(rms_norm(h, attn_norm[j]), w_qkv[j], w_o_attn[j])
            if v_first is None:
                v_first = v_layer
        else:
            mix = rwkv7_time_mix(rms_norm(h, rwkv_norm[j]), v_first, rwkv_mu[j], w_rkv[j], w_o_rwkv[j],
                                 w0[j], w1[j], w2[j], a0[j], a1[j], a2[j], v0[j], v1[j], v2[j],
                                 g1[j], g2[j], k_k[j], k_a[j], r_k[j], ln_x_w[j], ln_x_b[j])
        h = h + mix
        h = h + swiglu(rms_norm(h, ffn_norm[i]), w_ffn_in[i], w_ffn_out[i])
    return rms_norm(h[:, N_META:], final_norm)


_drawn_inputs = setup_inputs


def setup_inputs(seed=0):
    import zlib

    import numpy as np

    out = dict(_drawn_inputs(seed))
    spreads = {}
    factors = {'w1': 2.951,
     'w2': 2.902,
     'a0': 3.776,
     'v0': 72.452,
     'k_k': 2.712,
     'ln_x_w': 2.853,
     'ln_x_b': 8.0,
     'v1': 2.739,
     'v2': 2.753}
    for name, (base, spread) in spreads.items():
        noise = np.random.default_rng([zlib.crc32(name.encode()), seed]).standard_normal(out[name].shape)
        drawn = base * np.exp(spread * noise) if base else spread * noise
        out[name] = jnp.asarray(drawn.astype(out[name].dtype))
    for name, factor in factors.items():
        out[name] = (out[name] * factor).astype(out[name].dtype)
    return out
```

```python
import math

import concourse.bass as bass
from concourse import mybir
from concourse.alu_op_type import AluOpType as ALU
from contextlib import ExitStack

F32 = mybir.dt.float32
F32R = mybir.dt.float32r
ACT = mybir.ActivationFunctionType
ds = bass.ds

P = 128
D = 1024
T = 528
META = 16
SEQ = T - META
KT = D // P
HALF = T // 2
DFF = 2816
FT = DFF // P
FHALF = FT // 2
H = 16
HD = 64
RMS_EPS = 1e-6
GN_EPS = 64e-5
MASKED = -1.0e30

INPUTS = ['x', 'meta_tokens', 'attn_norm', 'w_qkv', 'w_o_attn', 'rwkv_norm', 'rwkv_mu', 'w_rkv', 'w_o_rwkv',
          'w0', 'w1', 'w2', 'a0', 'a1', 'a2', 'v0', 'v1', 'v2', 'g1', 'g2', 'k_k', 'k_a', 'r_k', 'ln_x_w', 'ln_x_b',
          'ffn_norm', 'w_ffn_in', 'w_ffn_out', 'final_norm']

VECTORS = [('attn_norm', 0), ('rwkv_norm', 0), ('mu', 0), ('mu', 1), ('mu', 2), ('mu', 3), ('mu', 4), ('mu', 5),
           ('w0', 0), ('a0', 0), ('v0', 0), ('k_k', 0), ('k_a', 0), ('r_k', 0), ('ln_x_w', 0), ('ln_x_b', 0),
           ('ffn_norm', 0), ('ffn_norm', 1), ('final_norm', 0)]


class State:
    pass


class Counter:

    def __init__(self, nc, ctx, name, start=0):
        self.h = ctx.enter_context(nc.semaphore(name))
        self.n = self.start = start


def flat(ap):
    return ap.rearrange("p a b -> p (a b)")


def setup(nc, d, ctx):
    k = State()
    k.nc, k.d, k.ctx = nc, d, ctx
    k.const_ready, k.in_loaded, k.tr_done, k.tr_copied, k.sq_ready = (
        Counter(nc, ctx, n) for n in ("const_ready", "in_loaded", "tr_done", "tr_copied", "sq_ready"))
    k.sum_ready, k.rs_step, k.xn_ready, k.xh_ready, k.xl_ready = (
        Counter(nc, ctx, n) for n in ("sum_ready", "rs_step", "xn_ready", "xh_ready", "xl_ready"))
    k.sig_ready, k.mh_ready, k.stored, k.sh_step, k.lora_read = (
        Counter(nc, ctx, n) for n in ("sig_ready", "mh_ready", "stored", "sh_step", "lora_read"))
    k.lora_done, k.hid_ready, k.vf_loaded, k.v_step, k.kn_raw = (
        Counter(nc, ctx, n) for n in ("lora_done", "hid_ready", "vf_loaded", "v_step", "kn_raw"))
    k.kn_ln, k.kn_exp, k.ka_step, k.b_ready, k.pads = (
        Counter(nc, ctx, n) for n in ("kn_ln", "kn_exp", "ka_step", "b_ready", "pads"))
    k.ml_ready, k.kn_clip, k.kn_sum, k.kn_used, k.state_ready = (
        Counter(nc, ctx, n, 1) for n in ("ml_ready", "kn_clip", "kn_sum", "kn_used", "state_ready"))
    k.sb = lambda name, shape, dt=F32: ctx.enter_context(nc.sbuf_tensor(name, shape, dt))
    k.sem = lambda name: Counter(nc, ctx, name)
    k.res = k.sb("res", [P, KT, T])
    k.raw = [k.sb(f"w_raw{j}", [P, FHALF, P]) for j in range(2)]
    k.ident = k.sb("ident", [P, P])
    k.ones = k.sb("ones", [P, P])
    k.vec = k.sb("vec", [P, len(VECTORS), KT])
    k.rstd = k.sb("rstd", [P, T])
    k.eps = k.sb("eps", [P, 3])
    k.psg = ctx.enter_context(nc.psum_tensor("psg", [P, 4, 512], F32))
    k.psx = ctx.enter_context(nc.psum_tensor("psx", [P, 4, 512], F32))
    k.raw_loaded = [k.sem(f"raw_loaded{j}") for j in range(2)]
    k.hi_ready = [k.sem(f"hi_ready{j}") for j in range(2)]
    k.lo_ready = [k.sem(f"lo_ready{j}") for j in range(2)]
    k.unit_done = [k.sem(f"unit_done{j}") for j in range(2)]
    k.psum_free = [Counter(nc, ctx, f"psum_free{j}", 1) for j in range(2)]
    k.bodies = 0
    return k


def operands(k, tmp, tag):
    k.x_hi = tmp.enter_context(k.nc.sbuf_tensor(f"x_hi{tag}", [P, KT, T], F32R))
    k.x_lo = tmp.enter_context(k.nc.sbuf_tensor(f"x_lo{tag}", [P, KT, T], F32R))
    k.w_hi = [tmp.enter_context(k.nc.sbuf_tensor(f"w_hi{tag}{j}", [P, FHALF, P], F32R)) for j in range(2)]
    k.w_lo = [tmp.enter_context(k.nc.sbuf_tensor(f"w_lo{tag}{j}", [P, FHALF, P], F32R)) for j in range(2)]


def vcol(k, name, which=0):
    n = VECTORS.index((name, which))
    return lambda m: k.vec[:, n, ds(m, 1)]



def load_unit(k, sp, j, src, kt):
    rows, _, cols = src.shape
    sp.dma_start(k.raw[j][0:rows, 0:kt, 0:cols], src).then_inc(k.raw_loaded[j].h, 16)


def split_hi(k, j, kt):
    k.nc.scalar.activation(k.w_hi[j][:, 0:kt, :], k.raw[j][:, 0:kt, :], ACT.Copy).then_inc(k.hi_ready[j].h, 1)


def split_lo(k, j, kt):
    k.nc.vector.tensor_tensor(k.w_lo[j][:, 0:kt, :], k.raw[j][:, 0:kt, :],
                              k.w_hi[j][:, 0:kt, :].bitcast(F32), ALU.subtract).then_inc(k.lo_ready[j].h, 1)


class Gemm:

    def __init__(self, src, kt, bodies, fresh=False):
        self.src, self.kt, self.bodies = src, kt, bodies
        self.fresh = fresh


def first_splits(k, g):
    @k.block.scalar
    def _(act):
        for j in range(2):
            act.wait_ge(k.raw_loaded[j].h, 16 * (k.bodies + 1))
            split_hi(k, j, g.kt)

    @k.block.vector
    def _(dve):
        for j in range(2):
            dve.wait_ge(k.hi_ready[j].h, k.bodies + 1)
            split_lo(k, j, g.kt)


def gemm_sync(k, sp, g, nxt):
    def load_body(i, at, stage):
        for j in range(2):
            sp.wait_ge(k.lo_ready[j].h, k.bodies + i + 1)
            load_unit(k, sp, j, stage.src(at, j), stage.kt)

    if g.bodies > 1:
        with sp.Fori(0, g.bodies - 1) as i:
            load_body(i, i + 1, g)
    if nxt is not None:
        load_body(g.bodies - 1, 0, nxt)


def gemm_scalar(k, act, g, nxt, epilogue):
    def body(i, kt):
        b = k.bodies + i
        for j in range(2):
            if kt:
                act.wait_ge(k.raw_loaded[j].h, 16 * (b + 2))
                act.wait_ge(k.unit_done[j].h, b + 1)
                split_hi(k, j, kt)
            epilogue(i, j)

    if g.bodies > 1:
        with act.Fori(0, g.bodies - 1) as i:
            body(i, g.kt)
    body(g.bodies - 1, nxt.kt if nxt is not None and not nxt.fresh else 0)


def gemm_vector(k, dve, g, nxt, epilogue):
    def body(i, kt):
        b = k.bodies + i
        for j in range(2):
            if kt:
                dve.wait_ge(k.hi_ready[j].h, b + 2)
                split_lo(k, j, kt)
            epilogue(i, j)

    if g.bodies > 1:
        with dve.Fori(0, g.bodies - 1) as i:
            body(i, g.kt)
    body(g.bodies - 1, nxt.kt if nxt is not None and not nxt.fresh else 0)


def gemm_tensor(k, pe, g, x_hi=None, x_lo=None, extra=None, before=None):
    x_hi, x_lo = x_hi or k.x_hi, x_lo or k.x_lo
    if before is not None:
        before()
    with pe.Fori(0, g.bodies) as i:
        b = k.bodies + i
        for j in range(2):
            pe.wait_ge(k.lo_ready[j].h, b + 1)
            pe.wait_ge(k.psum_free[j].h, b + 1)
            for half in range(2):
                out = k.psg[:, 2 * j + half, 0:HALF]
                cols = slice(half * HALF, half * HALF + HALF)
                for t in range(g.kt):
                    hi, lo = x_hi[:, t, cols], x_lo[:, t, cols]
                    for n, (w, x) in enumerate(((k.w_hi[j], hi), (k.w_hi[j], lo), (k.w_lo[j], hi))):
                        last = k.nc.tensor.matmul(out, w[:, t, :], x, start=t == 0 and n == 0,
                                                  stop=t == g.kt - 1 and n == 2)
            last.then_inc(k.unit_done[j].h, 1)
            if extra is not None:
                extra(i, j)


def halves(k, j):
    return k.psg[:, 2 * j:2 * j + 2, 0:HALF]


def as_halves(ap):
    return ap.rearrange("p o (a b) -> p (o a) b", a=2)



def load_tokens(k, first):
    nc, d = k.nc, k.d
    with ExitStack() as tmp, nc.Block() as block:
        k.block = block
        tok = tmp.enter_context(nc.sbuf_tensor("tok", [P, 5, D], F32))
        rows = tmp.enter_context(nc.sbuf_tensor("rows", [P, 2, P], F32))
        nv = len(VECTORS)
        groups = [(0, META, 0)] + [(META + P * g, P, g + 1) for g in range(4)]

        @block.gpsimd
        def _(pool):
            for c in (*k.psum_free, k.ml_ready, k.kn_clip, k.kn_sum, k.kn_used, k.state_ready):
                pool.sem_inc(c.h, c.start)
            nc.gpsimd.memset(k.ident[:], 0.0).then_inc(k.const_ready.h, 1)
            nc.gpsimd.memset(k.ones[:], 1.0).then_inc(k.const_ready.h, 1)
            nc.gpsimd.memset(k.eps[:, 0:1], RMS_EPS).then_inc(k.const_ready.h, 1)
            nc.gpsimd.memset(k.eps[:, 1:2], 1.0).then_inc(k.const_ready.h, 1)
            nc.gpsimd.memset(k.eps[:, 2:3], GN_EPS).then_inc(k.const_ready.h, 1)
            pool.wait_ge(k.const_ready.h, 5)
            nc.gpsimd.affine_select(out=k.ident[:], in_=k.ident[:], compare_op=ALU.not_equal, fill=1.0, base=0,
                                    pattern=[[-1, P]], channel_multiplier=1).then_inc(k.const_ready.h, 1)

        @block.sync
        def _(sp):
            sp.dma_start(tok[0:META, 0, :], d['meta_tokens']).then_inc(k.in_loaded.h, 16)
            sp.dma_start(tok[:, 1:5, :], d['x'][0].rearrange("(g p) f -> p g f", p=P)).then_inc(k.in_loaded.h, 16)
            for n, (name, which) in enumerate(VECTORS):
                src = d['rwkv_mu'][0] if name == 'mu' else d[name]
                if name == 'final_norm':
                    src = src.rearrange("(a f) -> a f", a=1)
                if name == 'r_k':
                    src = src.rearrange("a h n -> a (h n)")
                r = n * KT
                sp.dma_start(rows[r % P:r % P + KT, r // P, :],
                             src[which:which + 1, :].rearrange("a (m p) -> (a m) p", p=P)).then_inc(k.in_loaded.h, 16)

        @block.tensor
        def _(pe):
            pe.wait_ge(k.const_ready.h, 6)
            pe.wait_ge(k.in_loaded.h, 16 * (2 + nv))
            for m in range(KT):
                if m >= 2:
                    pe.wait_ge(k.tr_copied.h, m - 1)
                for at, size, g in groups:
                    bank, col = (m % 2) * 2 + (g == 4), (0 if g == 4 else at)
                    last = nc.tensor.transpose(k.psg[:, bank, col:col + size], tok[0:size, g, m * P:m * P + P],
                                               k.ident[0:size, 0:size])
                last.then_inc(k.tr_done.h, 1)
            left = nv * KT - P
            nc.tensor.transpose(k.psx[:, 0, 0:P], rows[:, 0, :], k.ident[:])
            nc.tensor.transpose(k.psx[:, 0, P:P + left], rows[0:left, 1, :],
                                k.ident[0:left, 0:left]).then_inc(k.tr_done.h, 1)

        @block.vector
        def _(dve):
            for m in range(KT):
                dve.wait_ge(k.tr_done.h, m + 1)
                cut = META + 3 * P
                nc.vector.tensor_copy(k.res[:, m, 0:cut], k.psg[:, (m % 2) * 2, 0:cut])
                nc.vector.tensor_copy(k.res[:, m, cut:T], k.psg[:, (m % 2) * 2 + 1, 0:P]).then_inc(k.tr_copied.h, 1)
            dve.wait_ge(k.tr_done.h, KT + 1)
            nc.vector.tensor_copy(flat(k.vec[:]), k.psx[:, 0, 0:nv * KT]).then_inc(k.tr_copied.h, 1)

        @block.sync
        def _(sp):
            for j in range(2):
                load_unit(k, sp, j, first.src(0, j), first.kt)

        first_splits(k, first)
    k.tr_done.n += KT + 1
    k.tr_copied.n += KT + 1


def norm_scalar(k, act, sq, split=True):
    nc = k.nc
    nc.scalar.preload_act_table_set("natural_log_exp_and_others")
    with act.Fori(0, KT) as m:
        nc.scalar.activation(sq[:, ds(m, 1), :], k.res[:, ds(m, 1), :], ACT.Square).then_inc(k.sq_ready.h, 1)
    act.wait_ge(k.sum_ready.h, k.sum_ready.n + 1)
    nc.scalar.activation(k.rstd[:].rearrange("p (a b) -> p a b", a=2), k.psx[:, 0:2, 0:HALF], ACT.Ln,
                         scale=1.0 / D, bias=k.eps[:, 0:1]).then_inc(k.rs_step.h, 1)
    act.wait_ge(k.rs_step.h, k.rs_step.n + 1)
    nc.scalar.activation(k.rstd[:], k.rstd[:], ACT.Exp, scale=-0.5).then_inc(k.rs_step.h, 1)
    if split:
        with act.Fori(0, KT) as m:
            act.wait_ge(k.xn_ready.h, k.xn_ready.n + m + 1)
            nc.scalar.activation(k.x_hi[:, ds(m, 1), :], sq[:, ds(m, 1), :], ACT.Copy).then_inc(k.xh_ready.h, 1)


def norm_tensor(k, pe, sq):
    def one(m, start, stop):
        pe.wait_ge(k.sq_ready.h, k.sq_ready.n + m + 1)
        for half in range(2):
            last = k.nc.tensor.matmul(k.psx[:, half, 0:HALF], k.ones[:], sq[:, ds(m, 1), half * HALF:(half + 1) * HALF],
                                      start=start, stop=stop)
        return last

    one(0, True, False)
    with pe.Fori(1, KT - 1) as m:
        one(m, False, False)
    one(KT - 1, False, True).then_inc(k.sum_ready.h, 1)


def norm_vector(k, dve, out, gain):
    dve.wait_ge(k.rs_step.h, k.rs_step.n + 2)
    with dve.Fori(0, KT) as m:
        k.nc.vector.scalar_tensor_tensor(out(m), k.res[:, ds(m, 1), :], gain(m), k.rstd[:].rearrange("p (o t) -> p o t", o=1),
                                         ALU.mult, ALU.mult).then_inc(k.xn_ready.h, 1)


def norm_stage(k, gain, fresh=None):
    nc = k.nc
    with ExitStack() as tmp, nc.Block() as block:
        sq = tmp.enter_context(nc.sbuf_tensor(f"sq{k.sq_ready.n}", [P, KT, T], F32))

        if fresh is not None:
            k.block = block
            first_splits(k, fresh)

        @block.scalar
        def _(act):
            norm_scalar(k, act, sq)

        @block.tensor
        def _(pe):
            norm_tensor(k, pe, sq)

        @block.vector
        def _(dve):
            norm_vector(k, dve, lambda m: sq[:, ds(m, 1), :], gain)

        @block.gpsimd
        def _(pool):
            with pool.Fori(0, KT) as m:
                pool.wait_ge(k.xh_ready.h, k.xh_ready.n + m + 1)
                nc.gpsimd.tensor_tensor(k.x_lo[:, ds(m, 1), :], sq[:, ds(m, 1), :],
                                        k.x_hi[:, ds(m, 1), :].bitcast(F32), ALU.subtract).then_inc(k.xl_ready.h, 1)
    for c in (k.sq_ready, k.xn_ready, k.xh_ready, k.xl_ready):
        c.n += KT
    k.sum_ready.n += 1
    k.rs_step.n += 2


def qkv_stage(k, g, nxt, qkv):
    nc = k.nc
    with nc.Block() as block:
        @block.sync
        def _(sp):
            gemm_sync(k, sp, g, nxt)

        @block.scalar
        def _(act):
            def epilogue(i, j):
                if j == 1:
                    act.wait_ge(k.unit_done[j].h, k.bodies + i + 1)
                    nc.scalar.activation(as_halves(qkv[:, ds(2 * i + j, 1), 0:T]), halves(k, j),
                                         ACT.Copy).then_inc(k.psum_free[j].h, 1)
            gemm_scalar(k, act, g, nxt, epilogue)

        @block.vector
        def _(dve):
            def epilogue(i, j):
                if j == 0:
                    dve.wait_ge(k.unit_done[j].h, k.bodies + i + 1)
                    nc.vector.tensor_scalar(as_halves(qkv[:, ds(2 * i + j, 1), 0:T]), halves(k, j), 1.0, None,
                                            ALU.mult).then_inc(k.psum_free[j].h, 1)
            gemm_vector(k, dve, g, nxt, epilogue)

        @block.tensor
        def _(pe):
            gemm_tensor(k, pe, g)
    k.bodies += g.bodies


def residual_stage(k, g, nxt, x_hi=None, x_lo=None):
    nc = k.nc
    with nc.Block() as block:
        @block.sync
        def _(sp):
            gemm_sync(k, sp, g, nxt)

        @block.scalar
        def _(act):
            gemm_scalar(k, act, g, nxt, lambda i, j: None)

        @block.vector
        def _(dve):
            def epilogue(i, j):
                dve.wait_ge(k.unit_done[j].h, k.bodies + i + 1)
                row = as_halves(k.res[:, ds(2 * i + j, 1), :])
                nc.vector.tensor_tensor(row, row, halves(k, j), ALU.add).then_inc(k.psum_free[j].h, 1)
            gemm_vector(k, dve, g, nxt, epilogue)

        @block.tensor
        def _(pe):
            gemm_tensor(k, pe, g, x_hi, x_lo)
    k.bodies += g.bodies


def ffn_in_stage(k, g, nxt, mid, m_hi, m_lo):
    nc = k.nc
    sig, prod = mid
    with nc.Block() as block:
        @block.sync
        def _(sp):
            gemm_sync(k, sp, g, nxt)

        @block.scalar
        def _(act):
            def epilogue(i, j):
                if j == 0:
                    act.wait_ge(k.unit_done[0].h, k.bodies + i + 1)
                    act.wait_ge(k.psum_free[0].h, k.bodies + i + 1)
                    nc.scalar.activation(sig[:], halves(k, 0), ACT.Sigmoid).then_inc(k.sig_ready.h, 1)
                else:
                    act.wait_ge(k.psum_free[1].h, k.bodies + i + 2)
                    nc.scalar.activation(as_halves(m_hi[:, ds(i, 1), :]), prod[:], ACT.Copy).then_inc(k.mh_ready.h, 1)
            gemm_scalar(k, act, g, nxt, epilogue)

        @block.vector
        def _(dve):
            def epilogue(i, j):
                if j == 0:
                    dve.wait_ge(k.sig_ready.h, k.sig_ready.n + i + 1)
                    dve.wait_ge(k.ml_ready.h, k.ml_ready.n + i)
                    nc.vector.tensor_tensor(prod[:], sig[:], halves(k, 0), ALU.mult).then_inc(k.psum_free[0].h, 1)
                else:
                    dve.wait_ge(k.psum_free[0].h, k.bodies + i + 2)
                    dve.wait_ge(k.unit_done[1].h, k.bodies + i + 1)
                    nc.vector.tensor_tensor(prod[:], prod[:], halves(k, 1), ALU.mult).then_inc(k.psum_free[1].h, 1)
            gemm_vector(k, dve, g, nxt, epilogue)

        @block.gpsimd
        def _(pool):
            with pool.Fori(0, g.bodies) as i:
                pool.wait_ge(k.mh_ready.h, k.mh_ready.n + i + 1)
                nc.gpsimd.tensor_tensor(as_halves(m_lo[:, ds(i, 1), :]), prod[:],
                                        as_halves(m_hi[:, ds(i, 1), :]).bitcast(F32),
                                        ALU.subtract).then_inc(k.ml_ready.h, 1)

        @block.tensor
        def _(pe):
            gemm_tensor(k, pe, g)
    for c in (k.sig_ready, k.mh_ready, k.ml_ready):
        c.n += g.bodies
    k.bodies += g.bodies


PIECES = [(0, 0, 512, 0, META), (1, 0, 400, 1, 128), (1, 400, 32, 0, 0), (2, 0, 272, 2, 256), (2, 272, 144, 3, 384),
          (2, 416, 16, 4, 512)]
BANK_AT = [0, 512, 944]
SCORES = 1376
NEAR = [(slice(0, 1), 512, slice(0, 512)), (slice(1, 3), 432, slice(512, SCORES))]
EXP_MAX = 40.0


def piece_cols(n, skip=0):
    bank, col, width, _, _ = PIECES[n]
    return slice(BANK_AT[bank] + col + skip, BANK_AT[bank] + col + width)


def attention_setup(k, qkv, vtok, neg, tri, minus, ident_r, ks):
    nc = k.nc
    with nc.Block() as block, ExitStack() as tmp:
        work = [tmp.enter_context(nc.sbuf_tensor(f"cst{n}", [P, P], F32)) for n in range(3)]
        made = k.sem("masks_made")
        v_saved = k.sem("v_saved")

        @block.gpsimd
        def _(pool):
            nc.gpsimd.memset(work[0][:], 0.0).then_inc(made.h, 1)
            nc.gpsimd.memset(work[1][:], -1.0).then_inc(made.h, 1)
            nc.gpsimd.memset(work[2][:], -1.0).then_inc(made.h, 1)
            nc.gpsimd.memset(vtok[:, 4, :], 0.0).then_inc(made.h, 1)
            nc.gpsimd.memset(ks[:, T:5 * P], 0.0).then_inc(made.h, 1)
            pool.wait_ge(made.h, 5)
            nc.gpsimd.affine_select(out=work[0][:], in_=work[0][:], compare_op=ALU.is_gt, fill=MASKED, base=0,
                                    pattern=[[1, P]], channel_multiplier=-1).then_inc(made.h, 1)
            nc.gpsimd.affine_select(out=work[1][:], in_=work[1][:], compare_op=ALU.is_ge, fill=0.0, base=0,
                                    pattern=[[-1, P]], channel_multiplier=1).then_inc(made.h, 1)
            pool.wait_ge(made.h, 7)
            nc.gpsimd.tensor_copy(neg[:], work[0][:])
            nc.gpsimd.tensor_copy(tri[:], work[1][:])
            nc.gpsimd.tensor_copy(minus[:], work[2][:])
            nc.gpsimd.tensor_copy(ident_r[:], k.ident[:]).then_inc(made.h, 1)

        @block.sync
        def _(sp):
            sp.dma_start(k.v_first, qkv[:, 2 * KT:3 * KT, :]).then_inc(v_saved.h, 16)
            sp.wait_ge(v_saved.h, 16)

        base = k.tr_done.n
        @block.tensor
        def _(pe):
            for m in range(KT):
                if m >= 2:
                    pe.wait_ge(k.tr_copied.h, k.tr_copied.n + m - 1)
                for g in range(5):
                    size = P if g < 4 else META
                    last = nc.tensor.transpose(k.psg[0:size, (m % 2) * 2 + (g == 4), (g % 4) * P:(g % 4) * P + P],
                                               qkv[:, 2 * KT + m, g * P:g * P + size], k.ident[:])
                last.then_inc(k.tr_done.h, 1)

        @block.vector
        def _(dve):
            dve.wait_ge(made.h, 8)
            for m in range(KT):
                dve.wait_ge(k.tr_done.h, k.tr_done.n + m + 1)
                nc.vector.tensor_copy(vtok[:, 0:4, m * P:m * P + P],
                                      k.psg[:, (m % 2) * 2, :].rearrange("p (g f) -> p g f", g=4))
                nc.vector.tensor_copy(vtok[0:META, 4, m * P:m * P + P],
                                      k.psg[0:META, (m % 2) * 2 + 1, 0:P]).then_inc(k.tr_copied.h, 1)
    k.tr_done.n += KT
    k.tr_copied.n += KT


def attention_stage(k, qkv):
    nc = k.nc
    with ExitStack() as tmp:
        def sb(name, shape, dt=F32):
            return tmp.enter_context(nc.sbuf_tensor(name, shape, dt))

        vtok = sb("vtok", [P, 5, D])
        neg, tri, minus, ident_r = (sb(n, [P, P], F32R) for n in ("neg", "tri", "minus", "ident_r"))
        qs, ks = sb("qs", [P, T]), sb("ks", [P, 5 * P])
        vs = [sb(f"vs{n}", [P, 5, HD]) for n in range(2)]
        rest = [sb(f"rest{n}", [P, SCORES]) for n in range(2)]
        rest_hi, rest_lo = sb("rest_hi", [P, SCORES], F32R), sb("rest_lo", [P, SCORES], F32R)
        att = [sb(f"att{n}", [P, SCORES]) for n in range(2)]
        attention_setup(k, qkv, vtok, neg, tri, minus, ident_r, ks)
        qk_staged, v_staged, z_done, clipped, exp_done, ln_ready = (
            k.sem(n) for n in ("qk_staged", "v_staged", "z_done", "clipped", "exp_done", "ln_ready"))
        rest_ready, rhi_ready, rlo_ready, later_done, att_ready, pv_done, ohi_ready, out_free = (
            k.sem(n) for n in ("rest_ready", "rhi_ready", "rlo_ready", "later_done", "att_ready", "pv_done",
                               "ohi_ready", "out_free"))
        zps = [k.psg, k.psx]
        out_main, out_meta = k.psg[:, 3, 0:SEQ], k.psx[:, 3, 0:META]
        PAIRS = H // 2

        def scores(n2, which):
            banks, width, _ = NEAR[which]
            return zps[n2][:, banks, 0:width]

        def part(t, which):
            banks, width, cols = NEAR[which]
            return t[:, cols].rearrange("p (a b) -> p a b", b=width)

        with nc.Block() as block:
            @block.gpsimd
            def _(pool):
                with pool.Fori(0, PAIRS) as i:
                    for hp in range(2):
                        for which in range(2):
                            pool.wait_ge(rhi_ready.h, 4 * i + 2 * hp + which + 1)
                            nc.gpsimd.tensor_tensor(part(rest_lo, which), part(rest[hp], which),
                                                    part(rest_hi, which).bitcast(F32),
                                                    ALU.subtract).then_inc(rlo_ready.h, 1)

            @block.tensor
            def _(pe):
                def z(i, hp):
                    rows = slice(HD * hp, HD * hp + HD)
                    ps = zps[hp]
                    for bank, col, width, key, t0 in PIECES:
                        nc.tensor.matmul(ps[:, bank, col:col + width], ks[rows, key * P:key * P + P],
                                         qs[rows, t0:t0 + width], start=col == 0, stop=True, skip_group_check=True)
                    for bank, col, width, key, t0 in PIECES:
                        skip = t0 - key * P
                        size = min(width, P - skip)
                        last = nc.tensor.matmul(ps[:, bank, col:col + size], ident_r[:], neg[:, skip:skip + size],
                                                start=False, stop=True, skip_group_check=True)
                    last.then_inc(z_done.h, 1)

                def later(i, hp):
                    n = 2 * i + hp
                    ps = zps[hp]
                    pe.wait_ge(rlo_ready.h, 2 * n + 2)
                    for a, (bank, col, width, key, t0) in enumerate(PIECES):
                        for r in (rest_hi, rest_lo):
                            last = nc.tensor.matmul(ps[:, bank, col:col + width], tri[:], r[:, piece_cols(a)],
                                                    start=False, stop=True, skip_group_check=True)
                    for a, (bank, col, width, key, t0) in enumerate(PIECES):
                        for c, (_, _, width2, key2, t2) in enumerate(PIECES):
                            if key2 > key and a != 2:
                                at = col + t2 - t0
                                for r in (rest_hi, rest_lo):
                                    last = nc.tensor.matmul(ps[:, bank, at:at + width2], minus[:], r[:, piece_cols(c)],
                                                            start=False, stop=True, skip_group_check=True)
                    last.then_inc(later_done.h, 1)

                def values(i, hp, first=False):
                    n = 2 * i + hp
                    pe.wait_ge(att_ready.h, 2 * n + 2)
                    pe.wait_ge(v_staged.h, n + 1)
                    if hp == 0 and not first:
                        pe.wait_ge(out_free.h, i)
                    rows = slice(HD * hp, HD * hp + HD)
                    for a, (bank, col, width, key, t0) in enumerate(PIECES):
                        if a != 2:
                            nc.tensor.matmul(out_main[rows, t0 - META:SEQ], vs[hp][:, key, :], att[hp][:, piece_cols(a)],
                                             start=a == 0, stop=a == 5)
                    cols = piece_cols(2)
                    nc.tensor.matmul(out_meta[rows, :], vs[hp][:, 0, :], att[hp][:, cols.start:cols.start + META],
                                     start=True, stop=True).then_inc(pv_done.h, 1)

                def body(i, first=False, last=False):
                    later(i, 0)
                    if not first:
                        values(i - 1, 1)
                    if not last:
                        pe.wait_ge(qk_staged.h, i + 2)
                        pe.wait_ge(att_ready.h, 4 * i + 2)
                        z(i + 1, 0)
                    later(i, 1)
                    values(i, 0, first)
                    if not last:
                        pe.wait_ge(att_ready.h, 4 * i + 4)
                        z(i + 1, 1)

                pe.wait_ge(qk_staged.h, 1)
                z(0, 0)
                z(0, 1)
                body(0, first=True)
                with pe.Fori(1, PAIRS - 1) as i:
                    body(i)
                body(PAIRS - 1, last=True)
                values(PAIRS - 1, 1)

            @block.vector
            def _(dve):
                def clip(n, hp):
                    dve.wait_ge(z_done.h, n + 1)
                    for which in range(2):
                        nc.vector.tensor_scalar(part(rest[hp], which), scores(hp, which), EXP_MAX, None,
                                                ALU.min).then_inc(clipped.h, 1)

                def softplus(n, hp):
                    for which in range(2):
                        dve.wait_ge(ln_ready.h, 2 * n + which + 1)
                        nc.vector.tensor_tensor(part(rest[hp], which), part(rest[hp], which), scores(hp, which),
                                                ALU.max).then_inc(rest_ready.h, 1)

                def stage_qk(i, first=False):
                    if not first:
                        dve.wait_ge(z_done.h, 2 * i)
                    nc.vector.tensor_scalar(qs[:].rearrange("p (o t) -> p o t", o=1), qkv[:, ds(i, 1), :], HD ** -0.5,
                                            None, ALU.mult)
                    nc.vector.tensor_scalar(ks[:, 0:T].rearrange("p (o t) -> p o t", o=1), qkv[:, ds(KT + i, 1), :],
                                            1.0, None, ALU.mult).then_inc(qk_staged.h, 1)

                def stage_v(i, hp, first):
                    if not first:
                        dve.wait_ge(pv_done.h, 2 * i - 1 + hp)
                    nc.vector.tensor_scalar(vs[hp][:], vtok[:, :, ds(i * P + hp * HD, HD)], 1.0, None,
                                            ALU.mult).then_inc(v_staged.h, 1)

                def out_low(i):
                    dve.wait_ge(ohi_ready.h, i + 1)
                    nc.vector.tensor_tensor(k.x_lo[:, ds(i, 1), 0:META], out_meta.rearrange("p (o t) -> p o t", o=1),
                                            k.x_hi[:, ds(i, 1), 0:META].bitcast(F32), ALU.subtract)
                    nc.vector.tensor_tensor(k.x_lo[:, ds(i, 1), META:T], out_main.rearrange("p (o t) -> p o t", o=1),
                                            k.x_hi[:, ds(i, 1), META:T].bitcast(F32),
                                            ALU.subtract).then_inc(out_free.h, 1)

                def body(i, first=False, last=False):
                    clip(2 * i, 0)
                    softplus(2 * i, 0)
                    if not last:
                        stage_qk(i + 1)
                    stage_v(i, 0, first)
                    clip(2 * i + 1, 1)
                    softplus(2 * i + 1, 1)
                    stage_v(i, 1, first)
                    if not first:
                        out_low(i - 1)

                stage_qk(0, first=True)
                body(0, first=True)
                with dve.Fori(1, PAIRS - 1) as i:
                    body(i)
                body(PAIRS - 1, last=True)
                out_low(PAIRS - 1)

            @block.scalar
            def _(act):
                def log_rest(n, hp):
                    for which in range(2):
                        act.wait_ge(clipped.h, 2 * n + which + 1)
                        nc.scalar.activation(part(rest[hp], which), part(rest[hp], which), ACT.Exp).then_inc(exp_done.h, 1)
                    for which in range(2):
                        act.wait_ge(exp_done.h, 2 * n + which + 1)
                        nc.scalar.activation(part(rest[hp], which), part(rest[hp], which), ACT.Ln,
                                             bias=k.eps[:, 1:2]).then_inc(ln_ready.h, 1)

                def rest_high(n, hp, first=False):
                    if not first:
                        act.wait_ge(later_done.h, n)
                    for which in range(2):
                        act.wait_ge(rest_ready.h, 2 * n + which + 1)
                        nc.scalar.activation(part(rest_hi, which), part(rest[hp], which), ACT.Copy).then_inc(rhi_ready.h, 1)

                def attend(n, hp, first=False):
                    act.wait_ge(later_done.h, n + 1)
                    if not first:
                        act.wait_ge(pv_done.h, n - 1)
                    for which in range(2):
                        nc.scalar.activation(part(att[hp], which), scores(hp, which), ACT.Exp).then_inc(att_ready.h, 1)

                def out_high(i):
                    act.wait_ge(pv_done.h, 2 * i + 2)
                    nc.scalar.activation(k.x_hi[:, ds(i, 1), 0:META], out_meta.rearrange("p (o t) -> p o t", o=1), ACT.Copy)
                    nc.scalar.activation(k.x_hi[:, ds(i, 1), META:T], out_main.rearrange("p (o t) -> p o t", o=1),
                                         ACT.Copy).then_inc(ohi_ready.h, 1)

                def body(i, first=False, last=False):
                    log_rest(2 * i + 1, 1)
                    attend(2 * i, 0, first)
                    if not first:
                        out_high(i - 1)
                    rest_high(2 * i + 1, 1)
                    if not last:
                        log_rest(2 * i + 2, 0)
                    attend(2 * i + 1, 1, first)
                    if not last:
                        rest_high(2 * i + 2, 0)

                nc.scalar.preload_act_table_set("natural_log_exp_and_others")
                log_rest(0, 0)
                rest_high(0, 0, first=True)
                body(0, first=True)
                with act.Fori(1, PAIRS - 1) as i:
                    body(i)
                body(PAIRS - 1, last=True)
                out_high(PAIRS - 1)



def columns(w, rows, at):
    r0, n = rows
    view = w[r0 * P:(r0 + n) * P, :].rearrange("(t p) c -> p t c", p=P)
    return lambda i, j: view[:, :, ds(at(i, j) * P, P)]


def ffn_gemms(d, n, fresh=False):
    out = []
    for half in range(2):
        w_in, w_out = d['w_ffn_in'][n], d['w_ffn_out'][n]
        out.append(Gemm(columns(w_in, (0, KT), lambda i, j, half=half: j * FT + half * FHALF + i), KT, FHALF,
                        fresh=fresh and half == 0))
        out.append(Gemm(columns(w_out, (half * FHALF, FHALF), lambda i, j: 2 * i + j), FHALF, KT // 2))
    return out


def ffn_layer(k, n, stages, nxt):
    norm_stage(k, vcol(k, 'ffn_norm', n), stages[0] if stages[0].fresh else None)
    with ExitStack() as tmp:
        m_hi, m_lo = (tmp.enter_context(k.nc.sbuf_tensor(f"mid_{n}{p}", [P, FHALF, T], F32R)) for p in ('hi', 'lo'))
        mid = [tmp.enter_context(k.nc.sbuf_tensor(f"{p}{n}", [P, 2, HALF], F32)) for p in ('sig', 'prod')]
        for half in range(2):
            follow = (stages + [nxt])[2 * half + 1:2 * half + 3]
            ffn_in_stage(k, stages[2 * half], follow[0], mid, m_hi, m_lo)
            residual_stage(k, stages[2 * half + 1], follow[1], m_hi, m_lo)


def build_program(nc, d, out):
    with ExitStack() as ctx:
        k = setup(nc, d, ctx)
        k.v_first = nc.dram_tensor("v_first", [P, KT, T], F32).ap()
        pair = lambda i, j: 2 * i + j
        g_qkv = Gemm(columns(d['w_qkv'][0], (0, KT), pair), KT, 3 * KT // 2)
        g_wo = Gemm(columns(d['w_o_attn'][0], (0, KT), pair), KT, KT // 2)
        g_ffn = [ffn_gemms(d, n, fresh=n == 1) for n in range(2)]
        lora = lora_gemms(d)
        with ExitStack() as era:
            operands(k, era, "a")
            load_tokens(k, g_qkv)
            norm_stage(k, vcol(k, 'attn_norm'))
            with ExitStack() as tmp:
                qkv = tmp.enter_context(nc.sbuf_tensor("qkv", [P, 3 * KT, T], F32))
                qkv_stage(k, g_qkv, g_wo, qkv)
                attention_stage(k, qkv)
            residual_stage(k, g_wo, g_ffn[0][0])
            ffn_layer(k, 0, g_ffn[0], lora['w'])
        rwkv_layer(k, d, lora, g_ffn[1])
        with ExitStack() as era:
            operands(k, era, "d")
            ffn_layer(k, 1, g_ffn[1], None)
        final_stage(k, out)


C = 64
CHUNKS = -(-T // C)
TP = CHUNKS * C
PAD = TP - T
DECAY = -math.exp(-0.5)
LEVELS = 6
LORA = {'w': ('w1', 'w2', 64), 'a': ('a1', 'a2', 64), 'v': ('v1', 'v2', 32)}
G_HALF = 80
LN_SHIFT = 20


def lora_gemms(d):
    out = {}
    for n, (first, second, rank) in LORA.items():
        out[n] = Gemm(lambda i, j, first=first, second=second:
                      d[first][0].rearrange("(t p) l -> p t l", p=P) if j == 0 else
                      d[second][0].rearrange("l (m c) -> l m c", c=P), KT, 1, fresh=n == 'w')
    out['g1'] = Gemm(lambda i, j: d['g1'][0][:, j * G_HALF:(j + 1) * G_HALF].rearrange("(t p) l -> p t l", p=P), KT, 1)
    out['g2'] = Gemm(lambda i, j: d['g2'][0][j * G_HALF:(j + 1) * G_HALF, :].rearrange("l (m c) -> l m c", c=P), KT, 1,
                     fresh=True)
    for n, which in (('r', 0), ('k', 1), ('v_big', 2)):
        out[n] = Gemm(columns(d['w_rkv'][0, which], (0, KT), lambda i, j: 2 * i + j), KT, KT // 2)
    out['wo'] = Gemm(columns(d['w_o_rwkv'][0], (0, KT), lambda i, j: 2 * i + j), KT, KT // 2)
    return out


def real(t, m):
    return t[:, ds(m, 1), PAD:TP].rearrange("p o (a b) -> p (o a) b", a=2)


def row(t, m, cols=slice(None)):
    return t[:, ds(m, 1), cols].rearrange("p o t -> p (o t)")


def shift_vector(k, dve, xn, tmp, mu):
    with dve.Fori(0, KT // 2) as i:
        for q in range(2):
            m = 2 * i + q
            dve.wait_ge(k.xl_ready.h, k.xl_ready.n + m - 1)
            k.nc.vector.tensor_tensor(tmp[q][:], row(xn, m, slice(0, T)), row(xn, m, slice(1, T + 1)),
                                      ALU.subtract).then_inc(k.sh_step.h, 1)
            dve.wait_ge(k.sh_step.h, k.sh_step.n + m + 1)
            k.nc.vector.scalar_tensor_tensor(tmp[q][:], tmp[q][:], mu(m), row(xn, m, slice(1, T + 1)),
                                             ALU.mult, ALU.add).then_inc(k.xn_ready.h, 1)


def shift_scalar(k, act, tmp):
    with act.Fori(0, KT // 2) as i:
        for q in range(2):
            m = 2 * i + q
            act.wait_ge(k.xn_ready.h, k.xn_ready.n + m + 1)
            k.nc.scalar.activation(row(k.x_hi, m), tmp[q][:], ACT.Copy).then_inc(k.xh_ready.h, 1)


def shift_gpsimd(k, pool, tmp):
    with pool.Fori(0, KT // 2) as i:
        for q in range(2):
            m = 2 * i + q
            pool.wait_ge(k.xh_ready.h, k.xh_ready.n + m + 1)
            k.nc.gpsimd.tensor_tensor(row(k.x_lo, m), tmp[q][:], row(k.x_hi, m).bitcast(F32),
                                      ALU.subtract).then_inc(k.xl_ready.h, 1)


def shift_wait(k, pe):
    pe.wait_ge(k.xl_ready.h, k.xl_ready.n + KT)


def shift_done(k):
    for c in (k.xn_ready, k.xh_ready, k.xl_ready, k.sh_step):
        c.n += KT


def lora_stage(k, g, nxt, r, mu, rank, func, bias, out, scan):
    nc = k.nc
    b = k.bodies

    def gemm_first(eng, j, split):
        if nxt is None or nxt.fresh:
            return
        if split is split_hi:
            eng.wait_ge(k.raw_loaded[j].h, 16 * (b + 2))
            eng.wait_ge(k.unit_done[j].h, b + 1)
        else:
            eng.wait_ge(k.hi_ready[j].h, b + 2)
        split(k, j, nxt.kt)

    with nc.Block() as block:
        @block.sync
        def _(sp):
            gemm_sync(k, sp, g, nxt)

        @block.tensor
        def _(pe):
            shift_wait(k, pe)
            pe.wait_ge(k.lo_ready[0].h, b + 1)
            pe.wait_ge(k.psum_free[0].h, b + 1)
            for half in range(2):
                cols = slice(half * HALF, half * HALF + HALF)
                for t in range(KT):
                    for n, (w, x) in enumerate(((k.w_hi, k.x_hi), (k.w_hi, k.x_lo), (k.w_lo, k.x_hi))):
                        last = nc.tensor.matmul(k.psg[:, half, 0:HALF], w[0][:, t, :], x[:, t, cols],
                                                start=t == 0 and n == 0, stop=t == KT - 1 and n == 2)
            last.then_inc(k.unit_done[0].h, 1)
            pe.wait_ge(k.lo_ready[1].h, b + 1)
            pe.wait_ge(k.psum_free[1].h, b + 2)
            for m in range(KT):
                if m >= 2:
                    pe.wait_ge(k.lora_read.h, k.lora_read.n + m - 1)
                for half in range(2):
                    cols = slice(half * HALF, half * HALF + HALF)
                    for n, (w, x) in enumerate(((k.w_hi, r.hid_hi), (k.w_hi, r.hid_lo), (k.w_lo, r.hid_hi))):
                        last = nc.tensor.matmul(k.psx[:, 2 * (m % 2) + half, 0:HALF], w[1][0:rank, m, :],
                                                x[0:rank, cols], start=n == 0, stop=n == 2)
                last.then_inc(k.lora_done.h if m < KT - 1 else k.unit_done[1].h, 1)

        @block.scalar
        def _(act):
            if g.fresh:
                for j in range(2):
                    act.wait_ge(k.raw_loaded[j].h, 16 * (b + 1))
                    split_hi(k, j, g.kt)
            shift_scalar(k, act, r.tmp)
            act.wait_ge(k.unit_done[0].h, b + 1)
            nc.scalar.activation(r.hid[0:rank, :].rearrange("p (a b) -> p a b", a=2), k.psg[0:rank, 0:2, 0:HALF],
                                 func).then_inc(k.psum_free[0].h, 1)
            act.wait_ge(k.psum_free[0].h, b + 2)
            nc.scalar.activation(r.hid_hi[0:rank, :], r.hid[0:rank, :], ACT.Copy).then_inc(k.hid_ready.h, 1)
            gemm_first(act, 0, split_hi)
            for m in range(KT):
                if m < KT - 1:
                    act.wait_ge(k.lora_done.h, k.lora_done.n + m + 1)
                else:
                    act.wait_ge(k.unit_done[1].h, b + 1)
                nc.scalar.activation(real(out, m), k.psx[:, 2 * (m % 2):2 * (m % 2) + 2, 0:HALF], ACT.Sigmoid,
                                     bias=bias(m).rearrange("p o -> p o")).then_inc(k.lora_read.h, 1)
            gemm_first(act, 1, split_hi)

        @block.vector
        def _(dve):
            if g.fresh:
                for j in range(2):
                    dve.wait_ge(k.hi_ready[j].h, b + 1)
                    split_lo(k, j, g.kt)
            shift_vector(k, dve, r.xn, r.tmp, mu)
            dve.wait_ge(k.hid_ready.h, k.hid_ready.n + 1)
            nc.vector.tensor_tensor(r.hid_lo[0:rank, :], r.hid[0:rank, :], r.hid_hi[0:rank, :].bitcast(F32),
                                    ALU.subtract).then_inc(k.psum_free[1].h, 1)
            gemm_first(dve, 0, split_lo)
            if scan:
                for m in range(KT):
                    dve.wait_ge(k.lora_read.h, k.lora_read.n + m + 1)
                    nc.vector.tensor_tensor_scan(out[:, m, :], r.reset[:], out[:, m, :], 0.0, ALU.mult, ALU.add)
            gemm_first(dve, 1, split_lo)

        @block.gpsimd
        def _(pool):
            shift_gpsimd(k, pool, r.tmp)
    shift_done(k)
    k.lora_read.n += KT
    k.lora_done.n += KT - 1
    k.hid_ready.n += 1
    k.bodies += 1


def g_hidden_stage(k, g, nxt, r, mu, g_hid):
    nc = k.nc
    b = k.bodies
    with nc.Block() as block:
        @block.sync
        def _(sp):
            gemm_sync(k, sp, g, nxt)
            sp.wait_ge(k.psum_free[0].h, b + 2)
            sp.wait_ge(k.psum_free[1].h, b + 2)
            sp.dma_start(g_hid, r.ghid[:]).then_inc(k.stored.h, 16)
            sp.wait_ge(k.stored.h, k.stored.n + 16)

        @block.tensor
        def _(pe):
            gemm_tensor(k, pe, g, before=lambda: shift_wait(k, pe))

        @block.scalar
        def _(act):
            shift_scalar(k, act, r.tmp)

            def epilogue(i, j):
                act.wait_ge(k.unit_done[j].h, b + 1)
                nc.scalar.activation(r.ghid[:, j, :].rearrange("p (a b) -> p a b", a=2),
                                     k.psg[0:G_HALF, 2 * j:2 * j + 2, 0:HALF], ACT.Sigmoid).then_inc(k.psum_free[j].h, 1)
            gemm_scalar(k, act, g, nxt, epilogue)

        @block.vector
        def _(dve):
            shift_vector(k, dve, r.xn, r.tmp, mu)
            gemm_vector(k, dve, g, nxt, lambda i, j: None)

        @block.gpsimd
        def _(pool):
            shift_gpsimd(k, pool, r.tmp)
    shift_done(k)
    k.stored.n += 16
    k.bodies += 1


def v_stage(k, g, nxt, r, mu):
    nc = k.nc
    b = k.bodies
    with nc.Block() as block:
        @block.sync
        def _(sp):
            gemm_sync(k, sp, g, nxt)

        @block.tensor
        def _(pe):
            gemm_tensor(k, pe, g)

        @block.scalar
        def _(act):
            gemm_scalar(k, act, g, nxt, lambda i, j: None)

        @block.vector
        def _(dve):
            dve.wait_ge(k.vf_loaded.h, 16)

            def epilogue(i, j):
                m = 2 * i + j
                n = k.v_step.n + 2 * m
                dve.wait_ge(k.unit_done[j].h, b + i + 1)
                nc.vector.tensor_tensor(real(r.vv, m), real(r.kk_in, m), halves(k, j), ALU.subtract).then_inc(k.v_step.h, 1)
                dve.wait_ge(k.v_step.h, n + 1)
                nc.vector.tensor_tensor(real(r.vv, m), real(r.vv, m), real(r.rr, m), ALU.mult).then_inc(k.v_step.h, 1)
                dve.wait_ge(k.v_step.h, n + 2)
                nc.vector.tensor_tensor(real(r.vv, m), real(r.vv, m), halves(k, j), ALU.add).then_inc(k.psum_free[j].h, 1)
            gemm_vector(k, dve, g, nxt, epilogue)
    k.v_step.n += 2 * KT
    k.bodies += g.bodies


def k_stage(k, g, nxt, r, mu):
    nc = k.nc
    b = k.bodies
    with nc.Block() as block:
        @block.sync
        def _(sp):
            gemm_sync(k, sp, g, nxt)

        @block.tensor
        def _(pe):
            gemm_tensor(k, pe, g, before=lambda: shift_wait(k, pe))

        @block.scalar
        def _(act):
            shift_scalar(k, act, r.tmp)

            def epilogue(i, j):
                act.wait_ge(k.unit_done[j].h, b + i + 1)
                nc.scalar.activation(real(r.kk_in, 2 * i + j), halves(k, j), ACT.Copy).then_inc(k.psum_free[j].h, 1)
            gemm_scalar(k, act, g, nxt, epilogue)

        @block.vector
        def _(dve):
            shift_vector(k, dve, r.xn, r.tmp, mu)
            gemm_vector(k, dve, g, nxt, lambda i, j: None)

        @block.gpsimd
        def _(pool):
            shift_gpsimd(k, pool, r.tmp)
    shift_done(k)
    k.bodies += g.bodies


def r_stage(k, g, nxt, r, mu):
    nc = k.nc
    b = k.bodies
    half_tp = TP // 2
    kkc, kac = vcol(k, 'k_k'), vcol(k, 'k_a')
    with nc.Block() as block:
        @block.sync
        def _(sp):
            gemm_sync(k, sp, g, nxt)

        @block.tensor
        def _(pe):
            def head_sums(i, j):
                m = 2 * i + j
                pe.wait_ge(k.sq_ready.h, k.sq_ready.n + m + 1)
                pe.wait_ge(k.kn_clip.h, k.kn_clip.n + m)
                for half in range(2):
                    last = nc.tensor.matmul(k.psx[:, half, 0:half_tp], r.heads[:],
                                            r.sq[:, half * half_tp:(half + 1) * half_tp], start=True, stop=True)
                last.then_inc(k.kn_sum.h, 1)
            gemm_tensor(k, pe, g, extra=head_sums, before=lambda: shift_wait(k, pe))

        @block.scalar
        def _(act):
            shift_scalar(k, act, r.tmp)

            def epilogue(i, j):
                m = 2 * i + j
                act.wait_ge(k.kn_raw.h, k.kn_raw.n + m + 1)
                act.wait_ge(k.kn_sum.h, k.kn_sum.n + m)
                nc.scalar.activation(r.sq[:], row(r.xn, m), ACT.Square).then_inc(k.sq_ready.h, 1)
                act.wait_ge(k.unit_done[j].h, b + i + 1)
                nc.scalar.activation(real(r.rr, m), halves(k, j), ACT.Copy).then_inc(k.psum_free[j].h, 1)
                act.wait_ge(k.kn_clip.h, k.kn_clip.n + m + 1)
                nc.scalar.activation(r.norm[:], r.norm[:], ACT.Ln, scale=2.0 ** LN_SHIFT).then_inc(k.kn_ln.h, 1)
                act.wait_ge(k.kn_ln.h, k.kn_ln.n + m + 1)
                nc.scalar.activation(r.norm[:], r.norm[:], ACT.Exp, scale=-0.5, bias=r.cst[:, 0:1]).then_inc(k.kn_exp.h, 1)
            gemm_scalar(k, act, g, nxt, epilogue)

        @block.vector
        def _(dve):
            shift_vector(k, dve, r.xn, r.tmp, mu)
            dve.wait_ge(k.xl_ready.h, k.xl_ready.n + KT)

            def epilogue(i, j):
                m = 2 * i + j
                nc.vector.tensor_scalar(row(r.xn, m), row(r.kk_in, m), kkc(m), None, ALU.mult).then_inc(k.kn_raw.h, 1)
                dve.wait_ge(k.kn_sum.h, k.kn_sum.n + m + 1)
                dve.wait_ge(k.kn_used.h, k.kn_used.n + m)
                nc.vector.tensor_scalar(r.norm[:].rearrange("p (a b) -> p a b", a=2), k.psx[:, 0:2, 0:half_tp],
                                        1e-24, None, ALU.max).then_inc(k.kn_clip.h, 1)
                nc.vector.tensor_scalar(r.ka[:], row(r.aa, m), kac(m), r.omka[:, ds(m, 1)], ALU.mult,
                                        ALU.add).then_inc(k.ka_step.h, 1)
                dve.wait_ge(k.ka_step.h, k.ka_step.n + m + 1)
                nc.vector.tensor_tensor(row(r.kk_in, m), row(r.kk_in, m), r.ka[:], ALU.mult)
                dve.wait_ge(k.kn_exp.h, k.kn_exp.n + m + 1)
                nc.vector.tensor_tensor(row(r.xn, m), row(r.xn, m), r.norm[:], ALU.mult).then_inc(k.kn_used.h, 1)
                dve.wait_ge(k.kn_used.h, k.kn_used.n + m + 1)
                nc.vector.tensor_tensor(row(r.aa, m), row(r.aa, m), row(r.xn, m), ALU.mult).then_inc(k.b_ready.h, 1)
            gemm_vector(k, dve, g, nxt, epilogue)

        @block.gpsimd
        def _(pool):
            shift_gpsimd(k, pool, r.tmp)
    shift_done(k)
    for c in (k.sq_ready, k.kn_clip, k.kn_sum, k.kn_raw, k.kn_ln, k.kn_exp, k.kn_used, k.ka_step):
        c.n += KT
    k.bodies += g.bodies


def chunk_masks(k, ch):
    nc = k.nc
    with nc.Block() as block:
        @block.gpsimd
        def _(pool):
            fills = [(ch.incl, 1.0), (ch.strict, 1.0), (ch.level_t, 0.0), (ch.eye, 0.0), (ch.vc, 0.0), (ch.state, 0.0)]
            fills += [(e, 0.0) for e in ch.level]
            for t, value in fills:
                nc.gpsimd.memset(t[:], value).then_inc(ch.mk.h, 1)
            n = len(fills)
            pool.wait_ge(ch.mk.h, n)
            nc.gpsimd.memset(ch.level_t[:].rearrange("p (g two) -> p g two", two=2)[:, :, 1], 1.0).then_inc(ch.mk.h, 1)
            for e, mask in enumerate(ch.level):
                view = mask[:].rearrange("p (g two w) -> p g two w", two=2, w=2 ** e)
                nc.gpsimd.memset(view[:, :, 0, :], 1.0).then_inc(ch.mk.h, 1)
            n += 1 + LEVELS
            pool.wait_ge(ch.mk.h, n)
            for hp in range(2):
                rows = slice(C * hp, C * hp + C)
                view = ch.level_t[rows, :].rearrange("p (g two) -> p g two", two=2)[:, :, 1]
                steps = [(ch.incl[rows, :], ALU.is_ge, 0.0, 0, [[1, C]], -1),
                         (ch.strict[rows, :], ALU.is_gt, 0.0, 0, [[1, C]], -1),
                         (ch.eye[rows, :], ALU.not_equal, 1.0, 0, [[1, C]], -1),
                         (view, ALU.is_equal, 0.0, 0, [[-2, C // 2]], 1)]
                for e, mask in enumerate(ch.level):
                    w = 2 ** e
                    view = mask[rows, :].rearrange("p (g two w) -> p g two w", two=2, w=w)[:, :, 0, :]
                    steps.append((view, ALU.is_ge, 0.0, -w, [[-2 * w, C // (2 * w)], [0, w]], 1))
                    steps.append((view, ALU.is_ge, 0.0, 2 * w - 1, [[2 * w, C // (2 * w)], [0, w]], -1))
                for view, op, fill, base, pattern, by in steps:
                    nc.gpsimd.affine_select(out=view, in_=view, compare_op=op, fill=fill, base=base, pattern=pattern,
                                            channel_multiplier=by).then_inc(ch.mk.h, 1)
                    n += 1
                    pool.wait_ge(ch.mk.h, n)

        @block.vector
        def _(dve):
            nc.vector.memset(ch.w_ext[:, :, 0:1], 1.0)


def chunk_stage(k, r):
    nc = k.nc
    with ExitStack() as tmp:
        def sb(name, shape, dt=F32):
            return tmp.enter_context(nc.sbuf_tensor(name, shape, dt))

        ch = State()
        ch.mk = k.sem("chunk_masks")
        ch.incl, ch.strict, ch.level_t, ch.eye = (sb(n, [P, C]) for n in ("incl", "strict", "level_t", "eye"))
        ch.level = [sb(f"level{e}", [P, C]) for e in range(LEVELS)]
        ch.w_ext, ch.w_inv = sb("w_ext", [P, KT, C + 1]), sb("w_inv", [P, KT, C])
        ch.vc, ch.state = sb("vc", [P, KT, 2, C]), sb("state", [P, KT, C])
        ar, bk, bkh, bkt = (sb(n, [P, KT, 2, C]) for n in ("ar", "bk", "bkh", "bkt"))
        uv, arm = sb("uv", [P, H, C]), sb("arm", [P, H, C])
        akm = sb("akm", [P, H, C])
        low, xs, xt, tt, wt, st_w, av = (sb(n, [P, KT, C]) for n in ("low", "xs", "xt", "tt", "wt", "st_w", "av"))
        es = [sb(f"es{n}", [P, KT, C]) for n in range(LEVELS - 1)]
        settled = k.sem("c_settled")
        chunk_masks(k, ch)
        (exps, prods, hats, vcp, trd, bkt_r, uvv_r, lps, low_r, e_r, x_r, quad, arm_r, t_d, t_r, dx_d, w_d, wt_r, u_d,
         u_r, y_d, s_d, stw_r, y_r, av_d, av_r) = (k.sem("c_" + n) for n in (
             "exps", "prods", "hats", "vcopied", "transposed", "bkt", "uvv", "lproduct", "low", "e", "x", "quad", "arm",
             "t_done", "t", "dx", "w_done", "w", "u_done", "u", "y_done", "s_done", "stw", "y", "av_done", "av"))
        ps = [k.psg[:, n, :].rearrange("p (m c) -> p m c", c=C) for n in range(4)]
        ps += [k.psx[:, n, :].rearrange("p (m c) -> p m c", c=C) for n in range(4)]
        heads = [(h, h // 2, slice(HD * (h % 2), HD * (h % 2) + HD)) for h in range(H)]

        def at(h):
            return (h % 2) * KT + h // 2

        def over_rows(mask):
            return mask[:].rearrange("p (o c) -> p o c", o=1).broadcast_to([P, KT, C])

        def chunk(t, c, first=0):
            return t[:, :, ds(c * C + first, C)]

        with nc.Block() as block:
            @block.scalar
            def _(act):
                with act.Fori(0, CHUNKS) as c:
                    act.wait_ge(k.state_ready.h, c + 1)
                    nc.scalar.activation(ch.w_ext[:, :, 1:C + 1], chunk(r.gs, c), ACT.Exp, scale=DECAY).then_inc(exps.h, 1)
                    nc.scalar.activation(ch.w_inv[:], chunk(r.gs, c), ACT.Exp, scale=-DECAY).then_inc(exps.h, 1)
                    nc.scalar.activation(ch.vc[:, :, 1, :], chunk(r.vv, c), ACT.Copy).then_inc(vcp.h, 1)
                    act.wait_ge(trd.h, c + 1)
                    nc.scalar.activation(bkt[:].rearrange("p m a c -> p (m a) c"),
                                         k.psx[:, 0:2, :].rearrange("p b (m c) -> p (b m) c", c=C),
                                         ACT.Copy).then_inc(bkt_r.h, 1)
                    act.wait_ge(lps.h, c + 1)
                    nc.scalar.activation(low[:], ps[1], ACT.Copy).then_inc(low_r.h, 1)
                    act.wait_ge(av_d.h, c + 1)
                    nc.scalar.activation(av[:], ps[7], ACT.Copy).then_inc(av_r.h, 1)
                    for e in range(LEVELS - 1):
                        act.wait_ge(t_d.h, (LEVELS - 1) * c + e + 1)
                        nc.scalar.activation(tt[:], ps[2], ACT.Copy).then_inc(t_r.h, 1)
                    act.wait_ge(u_d.h, c + 1)
                    nc.scalar.activation(uv[0:C, :, :], k.psx[0:C, 0:2, :].rearrange("p b (m c) -> p (b m) c", c=C),
                                         ACT.Copy).then_inc(u_r.h, 1)

            @block.gpsimd
            def _(pool):
                with pool.Fori(0, CHUNKS) as c:
                    pool.wait_ge(low_r.h, c + 1)
                    for e in range(LEVELS - 1):
                        nc.gpsimd.tensor_tensor(es[e][:], low[:], over_rows(ch.level[e + 1]), ALU.mult).then_inc(e_r.h, 1)
                    nc.gpsimd.tensor_tensor(st_w[:], ch.state[:], ch.w_ext[:, :, C:C + 1].broadcast_to([P, KT, C]),
                                            ALU.mult).then_inc(stw_r.h, 1)

            @block.vector
            def _(dve):
                with dve.Fori(0, CHUNKS) as c:
                    dve.wait_ge(exps.h, 2 * c + 2)
                    nc.vector.tensor_tensor(bk[:, :, 0, :], chunk(r.aa, c), ch.w_inv[:], ALU.mult)
                    nc.vector.tensor_tensor(bk[:, :, 1, :], chunk(r.kk_in, c), ch.w_inv[:], ALU.mult).then_inc(prods.h, 1)
                    nc.vector.tensor_tensor(ar[:, :, 0, :], chunk(r.xn, c), ch.w_ext[:, :, 0:C], ALU.mult)
                    nc.vector.tensor_tensor(ar[:, :, 1, :], chunk(r.rr, c), ch.w_ext[:, :, 1:C + 1],
                                            ALU.mult).then_inc(prods.h, 1)
                    dve.wait_ge(prods.h, 2 * c + 1)
                    nc.vector.tensor_tensor(bkh[:].rearrange("p m a c -> p m (a c)"), bk[:].rearrange("p m a c -> p m (a c)"),
                                            ch.w_ext[:, :, C:C + 1].broadcast_to([P, KT, 2 * C]), ALU.mult).then_inc(hats.h, 1)
                    dve.wait_ge(trd.h, c + 1)
                    nc.vector.tensor_copy(uv[C:P, :, :].rearrange("p (two m) c -> p m two c", two=2),
                                          k.psx[C:P, 2:4, :].rearrange("p b (m two c) -> p (b m) two c", two=2, c=C))\
                        .then_inc(uvv_r.h, 1)
                    dve.wait_ge(low_r.h, c + 1)
                    nc.vector.scalar_tensor_tensor(xs[:], low[:], -1.0, over_rows(ch.level[0]), ALU.mult, ALU.mult)\
                        .then_inc(x_r.h, 1)
                    nc.vector.scalar_tensor_tensor(xt[:], ps[0], -1.0, over_rows(ch.level_t), ALU.mult, ALU.mult)\
                        .then_inc(x_r.h, 1)
                    n = (2 * LEVELS + 1) * c
                    dve.wait_ge(x_r.h, n + 2)
                    nc.vector.tensor_tensor(xs[:], xs[:], over_rows(ch.eye), ALU.add)
                    nc.vector.tensor_tensor(xt[:], xt[:], over_rows(ch.eye), ALU.add).then_inc(x_r.h, 1)
                    dve.wait_ge(quad.h, c + 1)
                    q = k.psx[:].rearrange("p b (h c) -> p (b h) c", c=2 * C)
                    nc.vector.tensor_tensor(akm[C:P, :, :], q[C:P, :, 0:C],
                                            ch.strict[C:P, :].rearrange("p (o c) -> p o c", o=1).broadcast_to([C, H, C]),
                                            ALU.mult)
                    nc.vector.tensor_tensor(arm[:], q[:, :, C:2 * C],
                                            ch.incl[:].rearrange("p (o c) -> p o c", o=1).broadcast_to([P, H, C]),
                                            ALU.mult).then_inc(arm_r.h, 1)
                    for e in range(LEVELS - 1):
                        dve.wait_ge(dx_d.h, (LEVELS - 1) * c + e + 1)
                        nc.vector.tensor_tensor(xt[:], xt[:], ps[0], ALU.subtract).then_inc(x_r.h, 1)
                        if e < LEVELS - 2:
                            nc.vector.tensor_tensor(xs[:], xs[:], ps[1], ALU.subtract).then_inc(x_r.h, 1)
                        else:
                            dve.sem_inc(x_r.h, 1)
                    dve.wait_ge(av_r.h, c + 1)
                    dve.wait_ge(w_d.h, c + 1)
                    nc.vector.scalar_tensor_tensor(wt[:], ps[3], -1.0, av[:], ALU.mult, ALU.subtract).then_inc(wt_r.h, 1)
                    dve.wait_ge(y_d.h, c + 1)
                    nc.vector.tensor_scalar(chunk(r.xn, c), ps[6], 1.0, None, ALU.mult).then_inc(y_r.h, 1)
                    dve.wait_ge(s_d.h, c + 1)
                    dve.wait_ge(stw_r.h, c + 1)
                    nc.vector.tensor_tensor(ch.state[:], st_w[:], ps[7], ALU.add).then_inc(k.state_ready.h, 1)

            @block.tensor
            def _(pe):
                mm = nc.tensor.matmul

                def settle():
                    pe.sem_inc(settled.h, 1)

                with pe.Fori(0, CHUNKS) as c:
                    pe.wait_ge(prods.h, 2 * c + 2)
                    settle()
                    for h, m, rows in heads:
                        mm(ps[0][rows, m, :], bk[rows, m, 0, :], ar[rows, m, 0, :], start=True, stop=True)
                    for h, m, rows in heads:
                        last = mm(ps[1][rows, m, :], ar[rows, m, 0, :], bk[rows, m, 0, :], start=True, stop=True)
                    last.then_inc(lps.h, 1)
                    pe.wait_ge(hats.h, c + 1)
                    pe.wait_ge(vcp.h, c + 1)
                    for m in range(KT):
                        nc.tensor.transpose(k.psx[:, m // 4, (m % 4) * P:(m % 4) * P + P],
                                            bkh[:, m, :, :].rearrange("p a c -> p (a c)"), k.ident[:])
                        last = nc.tensor.transpose(k.psx[:, 2 + m // 4, (m % 4) * P:(m % 4) * P + P],
                                                   ch.vc[:, m, :, :].rearrange("p a c -> p (a c)"), k.ident[:])
                    last.then_inc(trd.h, 1)
                    pe.wait_ge(bkt_r.h, c + 1)
                    pe.wait_ge(uvv_r.h, c + 1)
                    settle()
                    for h, m, rows in heads:
                        last = mm(k.psx[:, 2 * (h % 2) + m // 4, (m % 4) * P:(m % 4) * P + P],
                                  bk[rows, m, :, :].rearrange("p a c -> p (a c)"),
                                  ar[rows, m, :, :].rearrange("p a c -> p (a c)"), start=True, stop=True)
                    last.then_inc(quad.h, 1)
                    pe.wait_ge(arm_r.h, c + 1)
                    settle()
                    for h, m, rows in heads:
                        last = mm(ps[7][rows, m, :], akm[C:P, at(h), :], uv[C:P, at(h), :], start=True, stop=True)
                    last.then_inc(av_d.h, 1)
                    for e in range(LEVELS - 1):
                        n = (LEVELS - 1) * c + e
                        pe.wait_ge(x_r.h, (2 * LEVELS + 1) * c + 3 + 2 * e)
                        pe.wait_ge(e_r.h, n + 1)
                        settle()
                        for h, m, rows in heads:
                            last = mm(ps[2][rows, m, :], es[e][rows, m, :], xt[rows, m, :], start=True, stop=True)
                        last.then_inc(t_d.h, 1)
                        pe.wait_ge(t_r.h, n + 1)
                        settle()
                        for h, m, rows in heads:
                            last = mm(ps[0][rows, m, :], xs[rows, m, :], tt[rows, m, :], start=True, stop=True)
                        if e < LEVELS - 2:
                            for h, m, rows in heads:
                                last = mm(ps[1][rows, m, :], tt[rows, m, :], xs[rows, m, :], start=True, stop=True)
                        last.then_inc(dx_d.h, 1)
                    pe.wait_ge(k.state_ready.h, c + 1)
                    settle()
                    for h, m, rows in heads:
                        last = mm(ps[3][rows, m, :], ar[rows, m, 0, :], ch.state[rows, m, :], start=True, stop=True)
                    last.then_inc(w_d.h, 1)
                    pe.wait_ge(wt_r.h, c + 1)
                    pe.wait_ge(x_r.h, (2 * LEVELS + 1) * (c + 1))
                    settle()
                    for h, m, rows in heads:
                        last = mm(ps[4 + h % 2][0:C, m, :], xt[rows, m, :], wt[rows, m, :], start=True, stop=True)
                    last.then_inc(u_d.h, 1)
                    pe.wait_ge(u_r.h, c + 1)
                    settle()
                    for h, m, rows in heads:
                        mm(ps[6][rows, m, :], ch.state[rows, m, :], ar[rows, m, 1, :], start=m == 0, stop=True,
                           skip_group_check=True)
                    for h, m, rows in heads:
                        last = mm(ps[6][rows, m, :], uv[:, at(h), :], arm[:, at(h), :], start=False, stop=True,
                                  skip_group_check=True)
                    last.then_inc(y_d.h, 1)
                    for h, m, rows in heads:
                        last = mm(ps[7][rows, m, :], bkt[:].rearrange("p m a c -> p m (a c)")[:, m, rows], uv[:, at(h), :],
                                  start=True, stop=True)
                    last.then_inc(s_d.h, 1)


def rwkv_layer(k, d, lora, g_ffn):
    nc = k.nc
    g_hid = nc.dram_tensor("g_hid", [G_HALF, 2, T], F32).ap()
    names = ('r', 'k', 'v', 'w', 'a', 'g')
    mus = {n: vcol(k, 'mu', i) for i, n in enumerate(names)}
    r = State()
    with ExitStack() as arrays:
        def sb(name, shape, dt=F32, where=arrays):
            return where.enter_context(nc.sbuf_tensor(name, shape, dt))
        r.heads = sb("heads", [P, P])
        r.gs, r.aa, r.vv, r.kk_in, r.rr, r.xn = (sb(n, [P, KT, TP]) for n in ("gs", "aa", "vv", "kk_in", "rr", "xn"))
        with ExitStack() as era:
            operands(k, era, "b")
            r.tmp = [sb(f"shifted{q}", [P, T], where=era) for q in range(2)]
            r.hid = sb("hid", [C, T], where=era)
            r.hid_hi, r.hid_lo = (sb(n, [C, T], F32R, where=era) for n in ("hid_hi", "hid_lo"))
            r.reset = sb("reset", [P, TP], where=era)
            r.ghid = sb("ghid", [G_HALF, 2, T], where=era)
            r.sq, r.norm, r.ka = r.reset, sb("norm", [P, TP], where=era), sb("ka", [P, TP], where=era)
            r.cst, r.omka = sb("cst_ln", [P, 1], where=era), sb("omka", [P, KT], where=era)
            rwkv_norm(k, r, vcol(k, 'rwkv_norm'))
            lora_stage(k, lora['w'], lora['a'], r, mus['w'], 64, ACT.Tanh, vcol(k, 'w0'), r.gs, True)
            lora_stage(k, lora['a'], lora['g1'], r, mus['a'], 64, ACT.Copy, vcol(k, 'a0'), r.aa, False)
            g_hidden_stage(k, lora['g1'], lora['v'], r, mus['g'], g_hid)
            lora_stage(k, lora['v'], lora['v_big'], r, mus['v'], 32, ACT.Copy, vcol(k, 'v0'), r.rr, False)
            v_stage(k, lora['v_big'], lora['k'], r, mus['v'])
            k_stage(k, lora['k'], lora['r'], r, mus['k'])
            r_stage(k, lora['r'], lora['g2'], r, mus['r'])
        chunk_stage(k, r)
        with ExitStack() as era:
            operands(k, era, "c")
            output_stage(k, lora['g2'], lora['wo'], r, g_hid)
            residual_stage(k, lora['wo'], g_ffn[0])


def rwkv_norm(k, r, gain):
    nc = k.nc
    with nc.Block() as block:
        @block.scalar
        def _(act):
            norm_scalar(k, act, r.vv[:, :, 0:T], split=False)

        @block.tensor
        def _(pe):
            norm_tensor(k, pe, r.vv[:, :, 0:T])

        @block.vector
        def _(dve):
            norm_vector(k, dve, lambda m: r.xn[:, ds(m, 1), 1:T + 1], gain)

        @block.sync
        def _(sp):
            sp.dma_start(r.kk_in[:, :, PAD:TP], k.v_first).then_inc(k.vf_loaded.h, 16)

        @block.gpsimd
        def _(pool):
            nc.gpsimd.memset(r.xn[:, :, 0:1], 0.0)
            nc.gpsimd.memset(r.heads[:], 0.0).then_inc(k.pads.h, 1)
            nc.gpsimd.memset(r.reset[:], 1.0).then_inc(k.pads.h, 1)
            nc.gpsimd.memset(r.cst[:], 0.5 * LN_SHIFT * math.log(2.0))
            for t in (r.gs, r.aa, r.kk_in, r.rr):
                nc.gpsimd.memset(t[:, :, 0:PAD], 0.0)
            pool.wait_ge(k.pads.h, 2)
            nc.gpsimd.memset(r.reset[:].rearrange("p (c t) -> p c t", t=C)[:, :, 0:1], 0.0)
            nc.gpsimd.memset(r.heads[0:HD, 0:HD], 1.0)
            n = VECTORS.index(('k_a', 0))
            nc.gpsimd.tensor_scalar(r.omka[:], k.vec[:, n, :], -1.0, 1.0, ALU.mult, ALU.add).then_inc(k.pads.h, 1)
            pool.wait_ge(k.pads.h, 3)
            nc.gpsimd.memset(r.heads[HD:P, HD:P], 1.0).then_inc(k.pads.h, 1)
            pool.wait_ge(k.pads.h, 4)
    with nc.Block() as block:
        @block.gpsimd
        def _(pool):
            nc.gpsimd.memset(r.vv[:, :, 0:PAD], 0.0)
    for c in (k.sq_ready, k.xn_ready):
        c.n += KT
    k.sum_ready.n += 1
    k.rs_step.n += 2


def output_stage(k, g, nxt, r, g_hid):
    nc = k.nc
    b = k.bodies
    y, prod, cent, sq, rs, bon, fin = r.xn, *(r.gs[:, n, 0:SEQ] for n in range(6))
    late = slice(C, TP)
    lnw, lnb, rk = vcol(k, 'ln_x_w'), vcol(k, 'ln_x_b'), vcol(k, 'r_k')
    prod_r, cent_r, sq_r, var_r, rs_r, bon_r, y_r, fin_r, sums, hid_in, hid_h, hid_l, zeroed = (
        k.sem("o_" + n) for n in ("prod", "cent", "sq", "var", "rs", "bonus", "y", "fin", "sums", "hid_in", "hid_hi",
                                  "hid_lo", "zeroed"))
    with ExitStack() as tmp, nc.Block() as block:
        hid = r.aa[0:G_HALF, 0:2, 0:T]
        hid_hi, hid_lo = (tmp.enter_context(nc.sbuf_tensor(f"ghid_{n}", [G_HALF, 2, T], F32R)) for n in ("hi", "lo"))

        @block.sync
        def _(sp):
            sp.dma_start(hid, g_hid).then_inc(hid_in.h, 16)
            gemm_sync(k, sp, g, nxt)

        @block.scalar
        def _(act):
            for j in range(2):
                act.wait_ge(k.raw_loaded[j].h, 16 * (b + 1))
                split_hi(k, j, g.kt)
            act.wait_ge(hid_in.h, 16)
            nc.scalar.activation(hid_hi[:], hid, ACT.Copy).then_inc(hid_h.h, 1)
            for m in range(KT):
                act.wait_ge(cent_r.h, m + 1)
                nc.scalar.activation(sq, cent, ACT.Square).then_inc(sq_r.h, 1)
                act.wait_ge(var_r.h, m + 1)
                nc.scalar.activation(rs, k.psx[:, 2, :], ACT.Ln, scale=1.0 / HD, bias=k.eps[:, 2:3]).then_inc(rs_r.h, 1)
                act.wait_ge(rs_r.h, 2 * m + 1)
                nc.scalar.activation(rs, rs, ACT.Exp, scale=-0.5).then_inc(rs_r.h, 1)
                act.wait_ge(fin_r.h, m + 1)
                nc.scalar.activation(k.x_hi[:, m, META:T], fin, ACT.Copy).then_inc(k.xh_ready.h, 1)
            for j in range(2):
                act.wait_ge(k.raw_loaded[j].h, 16 * (b + 2))
                act.wait_ge(k.unit_done[j].h, b + 1)
                split_hi(k, j, nxt.kt)

        @block.vector
        def _(dve):
            for j in range(2):
                dve.wait_ge(k.hi_ready[j].h, b + 1)
                split_lo(k, j, g.kt)
            dve.wait_ge(hid_h.h, 1)
            nc.vector.tensor_tensor(hid_lo[:], hid, hid_hi[:].bitcast(F32), ALU.subtract).then_inc(hid_l.h, 1)
            for m in range(KT):
                nc.vector.scalar_tensor_tensor(prod, r.rr[:, m, late], rk(m), r.kk_in[:, m, late], ALU.mult,
                                               ALU.mult).then_inc(prod_r.h, 1)
                dve.wait_ge(sums.h, m + 1)
                nc.vector.scalar_tensor_tensor(cent, k.psx[:, 1, :], -1.0 / HD, y[:, m, late], ALU.mult,
                                               ALU.add).then_inc(cent_r.h, 1)
                nc.vector.tensor_tensor(bon, k.psx[:, 0, :], r.vv[:, m, late], ALU.mult).then_inc(bon_r.h, 1)
                dve.wait_ge(rs_r.h, 2 * m + 2)
                nc.vector.scalar_tensor_tensor(cent, cent, lnw(m), rs, ALU.mult, ALU.mult).then_inc(y_r.h, 1)
                dve.wait_ge(y_r.h, 2 * m + 1)
                nc.vector.scalar_tensor_tensor(cent, cent, lnb(m), bon, ALU.add, ALU.add).then_inc(y_r.h, 1)
                dve.wait_ge(y_r.h, 2 * m + 2)
                dve.wait_ge(k.xl_ready.h, k.xl_ready.n + m)
                nc.vector.tensor_tensor(fin, cent, k.psx[:, 3, :], ALU.mult).then_inc(fin_r.h, 1)
            for j in range(2):
                dve.wait_ge(k.hi_ready[j].h, b + 2)
                split_lo(k, j, nxt.kt)

        @block.gpsimd
        def _(pool):
            nc.gpsimd.memset(k.x_hi[:, :, 0:META].bitcast(F32), 0.0)
            nc.gpsimd.memset(k.x_lo[:, :, 0:META].bitcast(F32), 0.0)
            for m in range(KT):
                pool.wait_ge(k.xh_ready.h, k.xh_ready.n + m + 1)
                nc.gpsimd.tensor_tensor(k.x_lo[:, m, META:T], fin, k.x_hi[:, m, META:T].bitcast(F32),
                                        ALU.subtract).then_inc(k.xl_ready.h, 1)

        @block.tensor
        def _(pe):
            for j in range(2):
                pe.wait_ge(k.lo_ready[j].h, b + 1)
            pe.wait_ge(hid_l.h, 1)
            for m in range(KT):
                pe.wait_ge(prod_r.h, m + 1)
                if m:
                    pe.wait_ge(fin_r.h, m)
                nc.tensor.matmul(k.psx[:, 1, :], r.heads[:], y[:, m, late], start=True, stop=True)
                nc.tensor.matmul(k.psx[:, 0, :], r.heads[:], prod, start=True, stop=True).then_inc(sums.h, 1)
                for j in range(2):
                    for n, (w, x) in enumerate(((k.w_hi, hid_hi), (k.w_hi, hid_lo), (k.w_lo, hid_hi))):
                        last = nc.tensor.matmul(k.psx[:, 3, :], w[j][0:G_HALF, m, :], x[:, j, META:T],
                                                start=j == 0 and n == 0, stop=j == 1 and n == 2)
                pe.wait_ge(sq_r.h, m + 1)
                nc.tensor.matmul(k.psx[:, 2, :], r.heads[:], sq, start=True, stop=True).then_inc(var_r.h, 1)
            last.then_inc(k.unit_done[0].h, 1)
            pe.wait_ge(fin_r.h, KT)
            pe.sem_inc(k.unit_done[1].h, 1)
            pe.sem_inc(k.psum_free[0].h, 1)
            pe.sem_inc(k.psum_free[1].h, 1)
    for c in (k.xh_ready, k.xl_ready):
        c.n += KT
    k.bodies += 1


def final_stage(k, out):
    nc = k.nc
    gain = vcol(k, 'final_norm')
    groups = SEQ // P
    with ExitStack() as tmp, nc.Block() as block:
        sq = tmp.enter_context(nc.sbuf_tensor("sq_final", [P, KT, T], F32))
        tok = tmp.enter_context(nc.sbuf_tensor("tok_out", [P, groups, D], F32))
        turned, copied = k.sem("turned"), k.sem("copied")

        @block.scalar
        def _(act):
            norm_scalar(k, act, sq, split=False)

        @block.vector
        def _(dve):
            norm_vector(k, dve, lambda m: sq[:, ds(m, 1), :], gain)
            for g in range(groups):
                for half in range(2):
                    n = 2 * g + half
                    dve.wait_ge(turned.h, n + 1)
                    nc.vector.tensor_copy(tok[:, g, half * 512:half * 512 + 512], k.psg[:, n % 4, :]).then_inc(copied.h, 1)

        @block.tensor
        def _(pe):
            norm_tensor(k, pe, sq)
            pe.wait_ge(k.xn_ready.h, k.xn_ready.n + KT)
            for g in range(groups):
                for half in range(2):
                    n = 2 * g + half
                    if n >= 4:
                        pe.wait_ge(copied.h, n - 3)
                    for q in range(4):
                        last = nc.tensor.transpose(k.psg[:, n % 4, q * P:q * P + P],
                                                   sq[:, 4 * half + q, META + g * P:META + g * P + P], k.ident[:])
                    last.then_inc(turned.h, 1)

        @block.sync
        def _(sp):
            view = out[0].rearrange("(g p) f -> g p f", p=P)
            for g in range(groups):
                sp.wait_ge(copied.h, 2 * g + 2)
                sp.dma_start(view[g], tok[:, g, :]).then_inc(k.stored.h, 16)
            sp.wait_ge(k.stored.h, k.stored.n + 16 * groups)



def kernel(**inputs):
    import numpy as np
    import concourse.bacc as bacc
    from concourse.bass_utils import run_bass_kernel_spmd

    nc = bacc.Bacc("TRN2", target_bir_lowering=False, num_devices=1, dynamic_dma_scratch_size=1024)
    arrays, d = {}, {}
    for name in INPUTS:
        a = np.ascontiguousarray(inputs[name])
        arrays[f"in_{name}_dram"] = a
        d[name] = nc.dram_tensor(f"in_{name}_dram", a.shape, mybir.dt.from_np(a.dtype), kind="ExternalInput").ap()
    out = nc.dram_tensor("out_0_dram", (1, SEQ, D), F32, kind="ExternalOutput").ap()
    build_program(nc, d, out)
    r = run_bass_kernel_spmd(nc, [arrays], core_ids=[0])
    return r.results[0]["out_0_dram"]
```

```python
import math

import concourse.bass as bass
from concourse import mybir
from concourse.alu_op_type import AluOpType as ALU
from contextlib import ExitStack

F32 = mybir.dt.float32
F32R = mybir.dt.float32r
ACT = mybir.ActivationFunctionType
ds = bass.ds

P = 128
D = 1024
T = 528
META = 16
SEQ = T - META
KT = D // P
HALF = T // 2
DFF = 2816
FT = DFF // P
FHALF = FT // 2
H = 16
HD = 64
RMS_EPS = 1e-6
GN_EPS = 64e-5
MASKED = -1.0e30
SHIFT_BUFFERS = 4

INPUTS = ['x', 'meta_tokens', 'attn_norm', 'w_qkv', 'w_o_attn', 'rwkv_norm', 'rwkv_mu', 'w_rkv', 'w_o_rwkv',
          'w0', 'w1', 'w2', 'a0', 'a1', 'a2', 'v0', 'v1', 'v2', 'g1', 'g2', 'k_k', 'k_a', 'r_k', 'ln_x_w', 'ln_x_b',
          'ffn_norm', 'w_ffn_in', 'w_ffn_out', 'final_norm']

VECTORS = [('attn_norm', 0), ('rwkv_norm', 0), ('mu', 0), ('mu', 1), ('mu', 2), ('mu', 3), ('mu', 4), ('mu', 5),
           ('w0', 0), ('a0', 0), ('v0', 0), ('k_k', 0), ('k_a', 0), ('r_k', 0), ('ln_x_w', 0), ('ln_x_b', 0),
           ('ffn_norm', 0), ('ffn_norm', 1), ('final_norm', 0)]


class State:
    pass


class Counter:

    def __init__(self, nc, ctx, name, start=0):
        self.h = ctx.enter_context(nc.semaphore(name))
        self.n = self.start = start


def flat(ap):
    return ap.rearrange("p a b -> p (a b)")


def setup(nc, d, ctx):
    k = State()
    k.nc, k.d = nc, d
    k.const_ready, k.in_loaded, k.tr_done, k.tr_copied, k.sq_ready = (
        Counter(nc, ctx, n) for n in ("const_ready", "in_loaded", "tr_done", "tr_copied", "sq_ready"))
    k.vec_loaded = Counter(nc, ctx, "vec_loaded")
    k.pair_ready, k.xl_even, k.xl_odd = (Counter(nc, ctx, n) for n in ("pair_ready", "xl_even", "xl_odd"))
    k.sum_ready, k.rs_step, k.xn_ready, k.xh_ready = (
        Counter(nc, ctx, n) for n in ("sum_ready", "rs_step", "xn_ready", "xh_ready"))
    k.sig_ready, k.mh_ready, k.stored, k.sh_step, k.lora_read = (
        Counter(nc, ctx, n) for n in ("sig_ready", "mh_ready", "stored", "sh_step", "lora_read"))
    k.lora_done, k.hid_ready, k.vf_loaded, k.v_step, k.kn_raw = (
        Counter(nc, ctx, n) for n in ("lora_done", "hid_ready", "vf_loaded", "v_step", "kn_raw"))
    k.kn_ln, k.kn_exp, k.ka_step, k.b_ready, k.pads = (
        Counter(nc, ctx, n) for n in ("kn_ln", "kn_exp", "ka_step", "b_ready", "pads"))
    k.ml_ready, k.kn_clip, k.kn_sum, k.kn_used = (
        Counter(nc, ctx, n, 1) for n in ("ml_ready", "kn_clip", "kn_sum", "kn_used"))
    k.xl_ready = Counter(nc, ctx, "xl_ready", SHIFT_BUFFERS)
    k.sb = lambda name, shape, dt=F32: ctx.enter_context(nc.sbuf_tensor(name, shape, dt))
    k.sem = lambda name: Counter(nc, ctx, name)
    k.res = k.sb("res", [P, KT, T])
    k.raw = [k.sb(f"w_raw{j}", [P, FHALF, P]) for j in range(2)]
    k.ident = k.sb("ident", [P, P])
    k.ones = k.sb("ones", [P, P])
    k.vec = k.sb("vec", [P, len(VECTORS), KT])
    k.rstd = k.sb("rstd", [P, T])
    k.eps = k.sb("eps", [P, 3])
    k.psg = ctx.enter_context(nc.psum_tensor("psg", [P, 4, 512], F32))
    k.psx = ctx.enter_context(nc.psum_tensor("psx", [P, 4, 512], F32))
    k.raw_loaded = [k.sem(f"raw_loaded{j}") for j in range(2)]
    k.hi_ready = [k.sem(f"hi_ready{j}") for j in range(2)]
    k.lo_ready = [k.sem(f"lo_ready{j}") for j in range(2)]
    k.unit_done = [k.sem(f"unit_done{j}") for j in range(2)]
    k.psum_free = [Counter(nc, ctx, f"psum_free{j}", 1) for j in range(2)]
    k.bodies = 0
    begin_at(k, 0)
    return k


def operands(k, tmp, tag):
    k.x_hi = tmp.enter_context(k.nc.sbuf_tensor(f"x_hi{tag}", [P, KT, T], F32R))
    k.x_lo = tmp.enter_context(k.nc.sbuf_tensor(f"x_lo{tag}", [P, KT, T], F32R))
    k.w_hi = [tmp.enter_context(k.nc.sbuf_tensor(f"w_hi{tag}{j}", [P, FHALF, P], F32R)) for j in range(2)]
    k.w_lo = [tmp.enter_context(k.nc.sbuf_tensor(f"w_lo{tag}{j}", [P, FHALF, P], F32R)) for j in range(2)]


def vcol(k, name, which=0):
    n = VECTORS.index((name, which))
    return lambda m: k.vec[:, n, ds(m, 1)]



def load_unit(k, sp, j, src, kt):
    rows, _, cols = src.shape
    sp.dma_start(k.raw[j][0:rows, 0:kt, 0:cols], src).then_inc(k.raw_loaded[j].h, 16)


def split_hi(k, j, kt):
    k.nc.scalar.activation(k.w_hi[j][:, 0:kt, :], k.raw[j][:, 0:kt, :], ACT.Copy).then_inc(k.hi_ready[j].h, 1)


def split_lo(k, j, kt):
    k.nc.vector.tensor_tensor(k.w_lo[j][:, 0:kt, :], k.raw[j][:, 0:kt, :],
                              k.w_hi[j][:, 0:kt, :].bitcast(F32), ALU.subtract).then_inc(k.lo_ready[j].h, 1)


class Gemm:

    def __init__(self, src, kt, bodies, fresh=False):
        self.src, self.kt, self.bodies = src, kt, bodies
        self.fresh = fresh


def gemm_sync(k, sp, g, nxt):
    def load_body(i, at, stage):
        for j in range(2):
            sp.wait_ge(k.lo_ready[j].h, k.bodies + i + 1)
            load_unit(k, sp, j, stage.src(at, j), stage.kt)

    if g.bodies > 1:
        with sp.Fori(0, g.bodies - 1) as i:
            load_body(i, i + 1, g)
    if nxt is not None:
        load_body(g.bodies - 1, 0, nxt)


def gemm_scalar(k, act, g, nxt, epilogue, before=None, split_first=False):
    def body(i, kt):
        b = k.bodies + i
        for j in range(2):
            if before is not None:
                before(i, j)
            if not split_first:
                epilogue(i, j)
            if kt:
                act.wait_ge(k.raw_loaded[j].h, 16 * (b + 2))
                act.wait_ge(k.unit_done[j].h, b + 1)
                split_hi(k, j, kt)
            if split_first:
                epilogue(i, j)

    if g.bodies > 1:
        with act.Fori(0, g.bodies - 1) as i:
            body(i, g.kt)
    body(g.bodies - 1, nxt.kt if nxt is not None and not nxt.fresh else 0)


def gemm_vector(k, dve, g, nxt, epilogue, before=None, split_first=False):
    def body(i, kt):
        b = k.bodies + i
        for j in range(2):
            if before is not None:
                before(i, j)
            if not split_first:
                epilogue(i, j)
            if kt:
                dve.wait_ge(k.hi_ready[j].h, b + 2)
                split_lo(k, j, kt)
            if split_first:
                epilogue(i, j)

    if g.bodies > 1:
        with dve.Fori(0, g.bodies - 1) as i:
            body(i, g.kt)
    body(g.bodies - 1, nxt.kt if nxt is not None and not nxt.fresh else 0)


def gemm_tensor(k, pe, g, x_hi=None, x_lo=None, extra=None, row_ready=None):
    x_hi, x_lo = x_hi or k.x_hi, x_lo or k.x_lo
    with pe.Fori(0, g.bodies) as i:
        b = k.bodies + i
        for j in range(2):
            pe.wait_ge(k.lo_ready[j].h, b + 1)
            pe.wait_ge(k.psum_free[j].h, b + 1)
            for half in range(2):
                out = k.psg[:, 2 * j + half, 0:k.half]
                cols = slice(k.t0 + half * k.half, k.t0 + (half + 1) * k.half)
                for t in range(g.kt):
                    if row_ready is not None and j == 0 and half == 0:
                        row_ready(pe, t)
                    hi, lo = x_hi[:, t, cols], x_lo[:, t, cols]
                    for n, (w, x) in enumerate(((k.w_hi[j], hi), (k.w_hi[j], lo), (k.w_lo[j], hi))):
                        last = k.nc.tensor.matmul(out, w[:, t, :], x, start=t == 0 and n == 0,
                                                  stop=t == g.kt - 1 and n == 2)
            last.then_inc(k.unit_done[j].h, 1)
            if extra is not None:
                extra(i, j)


def halves(k, j):
    return k.psg[:, 2 * j:2 * j + 2, 0:k.half]


def begin_at(k, t0):
    k.t0, k.half = t0, (T - t0) // 2


def as_halves(ap):
    return ap.rearrange("p o (a b) -> p (o a) b", a=2)


def live(k, ap, m):
    return as_halves(ap[:, ds(m, 1), k.t0:T])



def load_tokens(k, first):
    nc, d = k.nc, k.d
    with ExitStack() as tmp, nc.Block() as block:
        tok = tmp.enter_context(nc.sbuf_tensor("tok", [P, 5, D], F32))
        rows = tmp.enter_context(nc.sbuf_tensor("rows", [P, 2, P], F32))
        nv = len(VECTORS)
        groups = [(0, META, 0)] + [(META + P * g, P, g + 1) for g in range(4)]

        @block.gpsimd
        def _(pool):
            for c in (*k.psum_free, k.ml_ready, k.kn_clip, k.kn_sum, k.kn_used, k.xl_ready):
                pool.sem_inc(c.h, c.start)
            nc.gpsimd.memset(k.ident[:], 0.0).then_inc(k.const_ready.h, 1)
            nc.gpsimd.memset(k.ones[:], 1.0).then_inc(k.const_ready.h, 1)
            nc.gpsimd.memset(k.eps[:, 0:1], RMS_EPS).then_inc(k.const_ready.h, 1)
            nc.gpsimd.memset(k.eps[:, 1:2], 1.0).then_inc(k.const_ready.h, 1)
            nc.gpsimd.memset(k.eps[:, 2:3], GN_EPS).then_inc(k.const_ready.h, 1)
            pool.wait_ge(k.const_ready.h, 5)
            nc.gpsimd.affine_select(out=k.ident[:], in_=k.ident[:], compare_op=ALU.not_equal, fill=1.0, base=0,
                                    pattern=[[-1, P]], channel_multiplier=1).then_inc(k.const_ready.h, 1)

        @block.sync
        def _(sp):
            sp.dma_start(tok[0:META, 0, :], d['meta_tokens']).then_inc(k.in_loaded.h, 16)
            sp.dma_start(tok[:, 1:5, :], d['x'][0].rearrange("(g p) f -> p g f", p=P)).then_inc(k.in_loaded.h, 16)

        @block.tensor
        def _(pe):
            pe.wait_ge(k.const_ready.h, 6)
            pe.wait_ge(k.in_loaded.h, 16 * 2)
            for m in range(KT):
                if m >= 2:
                    pe.wait_ge(k.tr_copied.h, m - 1)
                for at, size, g in groups:
                    bank, col = (m % 2) * 2 + (g == 4), (0 if g == 4 else at)
                    last = nc.tensor.transpose(k.psg[:, bank, col:col + size], tok[0:size, g, m * P:m * P + P],
                                               k.ident[0:size, 0:size])
                last.then_inc(k.tr_done.h, 1)
            left = nv * KT - P
            pe.wait_ge(k.vec_loaded.h, 16 * nv)
            nc.tensor.transpose(k.psx[:, 0, 0:P], rows[:, 0, :], k.ident[:])
            nc.tensor.transpose(k.psx[:, 0, P:P + left], rows[0:left, 1, :],
                                k.ident[0:left, 0:left]).then_inc(k.tr_done.h, 1)

        @block.vector
        def _(dve):
            for m in range(KT):
                dve.wait_ge(k.tr_done.h, m + 1)
                cut = META + 3 * P
                nc.vector.tensor_copy(k.res[:, m, 0:cut], k.psg[:, (m % 2) * 2, 0:cut])
                nc.vector.tensor_copy(k.res[:, m, cut:T], k.psg[:, (m % 2) * 2 + 1, 0:P]).then_inc(k.tr_copied.h, 1)
            first_lo(k, dve, first)
            dve.wait_ge(k.tr_done.h, KT + 1)
            nc.vector.tensor_copy(flat(k.vec[:]), k.psx[:, 0, 0:nv * KT]).then_inc(k.tr_copied.h, 1)

        @block.sync
        def _(sp):
            for j in range(2):
                load_unit(k, sp, j, first.src(0, j), first.kt)

        @block.scalar
        def _(act):
            for n, (name, which) in enumerate(VECTORS):
                src = d['rwkv_mu'][0] if name == 'mu' else d[name]
                if name == 'final_norm':
                    src = src.rearrange("(a f) -> a f", a=1)
                if name == 'r_k':
                    src = src.rearrange("a h n -> a (h n)")
                r = n * KT
                act.dma_start(rows[r % P:r % P + KT, r // P, :],
                             src[which:which + 1, :].rearrange("a (m p) -> (a m) p", p=P)).then_inc(k.vec_loaded.h, 16)
            first_hi(k, act, first)
    k.tr_done.n += KT + 1
    k.tr_copied.n += KT + 1


def first_hi(k, act, g):
    for j in range(2):
        act.wait_ge(k.raw_loaded[j].h, 16 * (k.bodies + 1))
        split_hi(k, j, g.kt)


def first_lo(k, dve, g):
    for j in range(2):
        dve.wait_ge(k.hi_ready[j].h, k.bodies + 1)
        split_lo(k, j, g.kt)


def norm_scalar(k, act, sq, split=True, fresh=None):
    nc = k.nc
    nc.scalar.preload_act_table_set("natural_log_exp_and_others")
    with act.Fori(0, KT) as m:
        nc.scalar.activation(sq[:, ds(m, 1), :], k.res[:, ds(m, 1), :], ACT.Square).then_inc(k.sq_ready.h, 1)
    if fresh is not None:
        first_hi(k, act, fresh)
    act.wait_ge(k.sum_ready.h, k.sum_ready.n + 1)
    nc.scalar.activation(k.rstd[:].rearrange("p (a b) -> p a b", a=2), k.psx[:, 0:2, 0:HALF], ACT.Ln,
                         scale=1.0 / D, bias=k.eps[:, 0:1]).then_inc(k.rs_step.h, 1)
    act.wait_ge(k.rs_step.h, k.rs_step.n + 1)
    nc.scalar.activation(k.rstd[:], k.rstd[:], ACT.Exp, scale=-0.5).then_inc(k.rs_step.h, 1)
    if split:
        with act.Fori(0, KT) as m:
            act.wait_ge(k.xn_ready.h, k.xn_ready.n + m + 1)
            nc.scalar.activation(k.x_hi[:, ds(m, 1), :], sq[:, ds(m, 1), :], ACT.Copy).then_inc(k.xh_ready.h, 1)


def norm_tensor(k, pe, sq):
    for m in range(0, KT, 2):
        pe.wait_ge(k.pair_ready.h, k.pair_ready.n + m // 2 + 1)
        for half in range(2):
            last = k.nc.tensor.matmul(k.psx[:, half, 0:HALF], k.ones[:], sq[:, m, half * HALF:(half + 1) * HALF],
                                      start=m == 0, stop=m == KT - 2)
    last.then_inc(k.sum_ready.h, 1)


def norm_pairs(k, dve, sq, fresh=None):
    for m in range(0, KT, 2):
        dve.wait_ge(k.sq_ready.h, k.sq_ready.n + m + 2)
        k.nc.vector.tensor_tensor(sq[:, m, :], sq[:, m, :], sq[:, m + 1, :], ALU.add).then_inc(k.pair_ready.h, 1)
    if fresh is not None:
        first_lo(k, dve, fresh)


def norm_vector(k, dve, sq, out, gain, fresh=None):
    norm_pairs(k, dve, sq, fresh)
    dve.wait_ge(k.rs_step.h, k.rs_step.n + 2)
    with dve.Fori(0, KT) as m:
        k.nc.vector.scalar_tensor_tensor(out(m), k.res[:, ds(m, 1), :], gain(m), k.rstd[:].rearrange("p (o t) -> p o t", o=1),
                                         ALU.mult, ALU.mult).then_inc(k.xn_ready.h, 1)


class Norm:

    def __init__(self, k, tmp, gain):
        self.k, self.gain = k, gain
        self.sq = tmp.enter_context(k.nc.sbuf_tensor(f"sq{k.sq_ready.n}", [P, KT, T], F32))

    def low(self, eng, m):
        k = self.k
        eng.wait_ge(k.xh_ready.h, k.xh_ready.n + m + 1)
        eng.tensor_tensor(k.x_lo[:, m, :], self.sq[:, m, :], k.x_hi[:, m, :].bitcast(F32), ALU.subtract)\
            .then_inc(k.xl_even.h if m % 2 == 0 else k.xl_odd.h, 1)

    def vector(self, dve, fresh):
        k = self.k
        norm_pairs(k, dve, self.sq, fresh)
        dve.wait_ge(k.rs_step.h, k.rs_step.n + 2)
        for m in range(KT):
            k.nc.vector.scalar_tensor_tensor(self.sq[:, m, :], k.res[:, m, :], self.gain(m), k.rstd[:], ALU.mult,
                                             ALU.mult).then_inc(k.xn_ready.h, 1)
            if m >= 2 and m % 2 == 0:
                self.low(k.nc.vector, m - 2)
        self.low(k.nc.vector, KT - 2)

    def gpsimd(self):
        for m in range(1, KT, 2):
            self.low(self.k.nc.gpsimd, m)

    def row_ready(self, pe, t):
        k = self.k
        which = k.xl_even if t % 2 == 0 else k.xl_odd
        pe.wait_ge(which.h, which.n + t // 2 + 1)

    def done(self):
        k = self.k
        for c in (k.sq_ready, k.xn_ready, k.xh_ready):
            c.n += KT
        for c in (k.xl_even, k.xl_odd):
            c.n += KT // 2
        k.pair_ready.n += KT // 2
        k.sum_ready.n += 1
        k.rs_step.n += 2


def qkv_stage(k, g, nxt, qkv, norm=None):
    nc = k.nc
    with nc.Block() as block:
        @block.sync
        def _(sp):
            gemm_sync(k, sp, g, nxt)

        @block.scalar
        def _(act):
            if norm is not None:
                norm_scalar(k, act, norm.sq, fresh=g if g.fresh else None)

            def epilogue(i, j):
                if j == 1:
                    act.wait_ge(k.unit_done[j].h, k.bodies + i + 1)
                    nc.scalar.activation(as_halves(qkv[:, ds(2 * i + j, 1), 0:T]), halves(k, j),
                                         ACT.Copy).then_inc(k.psum_free[j].h, 1)
            gemm_scalar(k, act, g, nxt, epilogue)

        @block.vector
        def _(dve):
            if norm is not None:
                norm.vector(dve, g if g.fresh else None)

            def epilogue(i, j):
                if j == 0:
                    dve.wait_ge(k.unit_done[j].h, k.bodies + i + 1)
                    nc.vector.tensor_scalar(as_halves(qkv[:, ds(2 * i + j, 1), 0:T]), halves(k, j), 1.0, None,
                                            ALU.mult).then_inc(k.psum_free[j].h, 1)
            gemm_vector(k, dve, g, nxt, epilogue)

        @block.gpsimd
        def _(pool):
            norm.gpsimd()

        @block.tensor
        def _(pe):
            if norm is not None:
                norm_tensor(k, pe, norm.sq)
            gemm_tensor(k, pe, g, row_ready=norm.row_ready if norm is not None else None)
    k.bodies += g.bodies
    if norm is not None:
        norm.done()


def residual_stage(k, g, nxt, x_hi=None, x_lo=None):
    nc = k.nc
    with nc.Block() as block:
        @block.sync
        def _(sp):
            gemm_sync(k, sp, g, nxt)

        @block.scalar
        def _(act):
            gemm_scalar(k, act, g, nxt, lambda i, j: None)

        @block.vector
        def _(dve):
            def epilogue(i, j):
                dve.wait_ge(k.unit_done[j].h, k.bodies + i + 1)
                row = live(k, k.res, 2 * i + j)
                nc.vector.tensor_tensor(row, row, halves(k, j), ALU.add).then_inc(k.psum_free[j].h, 1)
            gemm_vector(k, dve, g, nxt, epilogue)

        @block.tensor
        def _(pe):
            gemm_tensor(k, pe, g, x_hi, x_lo)
    k.bodies += g.bodies


def ffn_in_stage(k, g, nxt, mid, m_hi, m_lo, norm=None):
    nc = k.nc
    sig, prod = (t[:, :, 0:k.half] for t in mid)
    with nc.Block() as block:
        @block.sync
        def _(sp):
            gemm_sync(k, sp, g, nxt)

        @block.scalar
        def _(act):
            if norm is not None:
                norm_scalar(k, act, norm.sq, fresh=g if g.fresh else None)

            def epilogue(i, j):
                if j == 0:
                    act.wait_ge(k.unit_done[0].h, k.bodies + i + 1)
                    act.wait_ge(k.psum_free[0].h, k.bodies + i + 1)
                    nc.scalar.activation(sig, halves(k, 0), ACT.Sigmoid).then_inc(k.sig_ready.h, 1)
                else:
                    act.wait_ge(k.psum_free[1].h, k.bodies + i + 2)
                    nc.scalar.activation(live(k, m_hi, i), prod, ACT.Copy).then_inc(k.mh_ready.h, 1)
            gemm_scalar(k, act, g, nxt, epilogue)

        @block.vector
        def _(dve):
            if norm is not None:
                norm.vector(dve, g if g.fresh else None)

            def epilogue(i, j):
                if j == 0:
                    dve.wait_ge(k.sig_ready.h, k.sig_ready.n + i + 1)
                    dve.wait_ge(k.ml_ready.h, k.ml_ready.n + i)
                    nc.vector.tensor_tensor(prod, sig, halves(k, 0), ALU.mult).then_inc(k.psum_free[0].h, 1)
                else:
                    dve.wait_ge(k.psum_free[0].h, k.bodies + i + 2)
                    dve.wait_ge(k.unit_done[1].h, k.bodies + i + 1)
                    nc.vector.tensor_tensor(prod, prod, halves(k, 1), ALU.mult).then_inc(k.psum_free[1].h, 1)
            gemm_vector(k, dve, g, nxt, epilogue)

        @block.gpsimd
        def _(pool):
            if norm is not None:
                norm.gpsimd()
            with pool.Fori(0, g.bodies) as i:
                pool.wait_ge(k.mh_ready.h, k.mh_ready.n + i + 1)
                nc.gpsimd.tensor_tensor(live(k, m_lo, i), prod,
                                        live(k, m_hi, i).bitcast(F32),
                                        ALU.subtract).then_inc(k.ml_ready.h, 1)

        @block.tensor
        def _(pe):
            if norm is not None:
                norm_tensor(k, pe, norm.sq)
            gemm_tensor(k, pe, g, row_ready=norm.row_ready if norm is not None else None)
    for c in (k.sig_ready, k.mh_ready, k.ml_ready):
        c.n += g.bodies
    k.bodies += g.bodies
    if norm is not None:
        norm.done()


PIECES = [(0, 0, 512, 0, META), (1, 0, 400, 1, 128), (1, 400, 32, 0, 0), (2, 0, 272, 2, 256), (2, 272, 144, 3, 384),
          (2, 416, 16, 4, 512)]
BANK_AT = [0, 512, 944]
SCORES = 1376
NEAR = [(slice(0, 1), 512, slice(0, 512)), (slice(1, 3), 432, slice(512, SCORES))]
EXP_MAX = 40.0


def piece_cols(n, skip=0):
    bank, col, width, _, _ = PIECES[n]
    return slice(BANK_AT[bank] + col + skip, BANK_AT[bank] + col + width)


def attention_setup(k, qkv, vtok, neg, tri, minus, ident_r, ks, qs, v_saved):
    nc = k.nc
    with nc.Block() as block, ExitStack() as tmp:
        work = [tmp.enter_context(nc.sbuf_tensor(f"cst{n}", [P, P], F32)) for n in range(3)]
        made = k.sem("masks_made")

        @block.gpsimd
        def _(pool):
            nc.gpsimd.memset(work[0][:], 0.0).then_inc(made.h, 1)
            nc.gpsimd.memset(work[1][:], -1.0).then_inc(made.h, 1)
            nc.gpsimd.memset(work[2][:], -1.0).then_inc(made.h, 1)
            nc.gpsimd.memset(vtok[:, 4, :], 0.0).then_inc(made.h, 1)
            nc.gpsimd.memset(ks[:, T:5 * P], 0.0).then_inc(made.h, 1)
            for q in qs:
                nc.gpsimd.memset(q[:], 0.0)
            pool.wait_ge(made.h, 5)
            nc.gpsimd.affine_select(out=work[0][:], in_=work[0][:], compare_op=ALU.is_gt, fill=MASKED, base=0,
                                    pattern=[[1, P]], channel_multiplier=-1).then_inc(made.h, 1)
            nc.gpsimd.affine_select(out=work[1][:], in_=work[1][:], compare_op=ALU.is_ge, fill=0.0, base=0,
                                    pattern=[[-1, P]], channel_multiplier=1).then_inc(made.h, 1)
            pool.wait_ge(made.h, 7)
            nc.gpsimd.tensor_copy(neg[:], work[0][:])
            nc.gpsimd.tensor_copy(tri[:], work[1][:])
            nc.gpsimd.tensor_copy(minus[:], work[2][:])
            nc.gpsimd.tensor_copy(ident_r[:], k.ident[:]).then_inc(made.h, 1)

        @block.sync
        def _(sp):
            sp.dma_start(k.v_first, qkv[:, 2 * KT:3 * KT, :]).then_inc(v_saved.h, 16)

        base = k.tr_done.n
        @block.tensor
        def _(pe):
            for m in range(KT):
                if m >= 2:
                    pe.wait_ge(k.tr_copied.h, k.tr_copied.n + m - 1)
                for g in range(5):
                    size = P if g < 4 else META
                    last = nc.tensor.transpose(k.psg[0:size, (m % 2) * 2 + (g == 4), (g % 4) * P:(g % 4) * P + P],
                                               qkv[:, 2 * KT + m, g * P:g * P + size], k.ident[:])
                last.then_inc(k.tr_done.h, 1)

        @block.vector
        def _(dve):
            dve.wait_ge(made.h, 8)
            for m in range(KT):
                dve.wait_ge(k.tr_done.h, k.tr_done.n + m + 1)
                nc.vector.tensor_copy(vtok[:, 0:4, m * P:m * P + P],
                                      k.psg[:, (m % 2) * 2, :].rearrange("p (g f) -> p g f", g=4))
                nc.vector.tensor_copy(vtok[0:META, 4, m * P:m * P + P],
                                      k.psg[0:META, (m % 2) * 2 + 1, 0:P]).then_inc(k.tr_copied.h, 1)
    k.tr_done.n += KT
    k.tr_copied.n += KT


def attention_stage(k, qkv):
    nc = k.nc
    with ExitStack() as tmp:
        def sb(name, shape, dt=F32):
            return tmp.enter_context(nc.sbuf_tensor(name, shape, dt))

        vtok = sb("vtok", [P, 5, D])
        neg, tri, minus, ident_r = (sb(n, [P, P], F32R) for n in ("neg", "tri", "minus", "ident_r"))
        qs, ks = [sb(f"qs{n}", [P, T]) for n in range(2)], sb("ks", [P, 5 * P])
        vs = [sb(f"vs{n}", [P, 5, HD]) for n in range(2)]
        rest = [sb(f"rest{n}", [P, SCORES]) for n in range(2)]
        rest_hi, rest_lo = sb("rest_hi", [P, SCORES], F32R), sb("rest_lo", [P, SCORES], F32R)
        att = [sb(f"att{n}", [P, SCORES]) for n in range(2)]
        v_saved = k.sem("v_saved")
        attention_setup(k, qkv, vtok, neg, tri, minus, ident_r, ks, qs, v_saved)
        qk_staged, v_staged, z_done, clipped, exp_done, ln_ready = (
            k.sem(n) for n in ("qk_staged", "v_staged", "z_done", "clipped", "exp_done", "ln_ready"))
        rest_ready, rhi_ready, rlo_ready, later_done, att_ready, pv_done, ohi_ready, out_free = (
            k.sem(n) for n in ("rest_ready", "rhi_ready", "rlo_ready", "later_done", "att_ready", "pv_done",
                               "ohi_ready", "out_free"))
        zps = [k.psg, k.psx]
        out_main, out_meta = k.psg[:, 3, 0:SEQ], k.psx[:, 3, 0:META]
        PAIRS = H // 2

        def scores(n2, which):
            banks, width, _ = NEAR[which]
            return zps[n2][:, banks, 0:width]

        def part(t, which):
            banks, width, cols = NEAR[which]
            return t[:, cols].rearrange("p (a b) -> p a b", b=width)

        with nc.Block() as block:
            @block.sync
            def _(sp):
                sp.wait_ge(v_saved.h, 16)

            @block.gpsimd
            def _(pool):
                with pool.Fori(0, PAIRS) as i:
                    for hp in range(2):
                        for which in range(2):
                            pool.wait_ge(rhi_ready.h, 4 * i + 2 * hp + which + 1)
                            nc.gpsimd.tensor_tensor(part(rest_lo, which), part(rest[hp], which),
                                                    part(rest_hi, which).bitcast(F32),
                                                    ALU.subtract).then_inc(rlo_ready.h, 1)

            @block.tensor
            def _(pe):
                def z(i, hp):
                    ps = zps[hp]
                    for bank, col, width, key, t0 in PIECES:
                        nc.tensor.matmul(ps[:, bank, col:col + width], ks[:, key * P:key * P + P],
                                         qs[hp][:, t0:t0 + width], start=col == 0, stop=True, skip_group_check=True)
                    for bank, col, width, key, t0 in PIECES:
                        skip = t0 - key * P
                        size = min(width, P - skip)
                        last = nc.tensor.matmul(ps[:, bank, col:col + size], ident_r[:], neg[:, skip:skip + size],
                                                start=False, stop=True, skip_group_check=True)
                    last.then_inc(z_done.h, 1)

                def later(i, hp):
                    n = 2 * i + hp
                    ps = zps[hp]
                    pe.wait_ge(rlo_ready.h, 2 * n + 2)
                    for a, (bank, col, width, key, t0) in enumerate(PIECES):
                        for r in (rest_hi, rest_lo):
                            last = nc.tensor.matmul(ps[:, bank, col:col + width], tri[:], r[:, piece_cols(a)],
                                                    start=False, stop=True, skip_group_check=True)
                    for a, (bank, col, width, key, t0) in enumerate(PIECES):
                        for c, (_, _, width2, key2, t2) in enumerate(PIECES):
                            if key2 > key and a != 2:
                                at = col + t2 - t0
                                for r in (rest_hi, rest_lo):
                                    last = nc.tensor.matmul(ps[:, bank, at:at + width2], minus[:], r[:, piece_cols(c)],
                                                            start=False, stop=True, skip_group_check=True)
                    last.then_inc(later_done.h, 1)

                def values(i, hp, first=False):
                    n = 2 * i + hp
                    pe.wait_ge(att_ready.h, 2 * n + 2)
                    pe.wait_ge(v_staged.h, n + 1)
                    if hp == 0 and not first:
                        pe.wait_ge(out_free.h, i)
                    rows = slice(HD * hp, HD * hp + HD)
                    for a, (bank, col, width, key, t0) in enumerate(PIECES):
                        if a != 2:
                            nc.tensor.matmul(out_main[rows, t0 - META:SEQ], vs[hp][:, key, :], att[hp][:, piece_cols(a)],
                                             start=a == 0, stop=a == 5)
                    cols = piece_cols(2)
                    nc.tensor.matmul(out_meta[rows, :], vs[hp][:, 0, :], att[hp][:, cols.start:cols.start + META],
                                     start=True, stop=True).then_inc(pv_done.h, 1)

                def body(i, first=False, last=False):
                    later(i, 0)
                    if not first:
                        values(i - 1, 1)
                    if not last:
                        pe.wait_ge(qk_staged.h, i + 2)
                        pe.wait_ge(att_ready.h, 4 * i + 2)
                        z(i + 1, 0)
                    later(i, 1)
                    values(i, 0, first)
                    if not last:
                        pe.wait_ge(att_ready.h, 4 * i + 4)
                        z(i + 1, 1)

                pe.wait_ge(qk_staged.h, 1)
                z(0, 0)
                z(0, 1)
                body(0, first=True)
                with pe.Fori(1, PAIRS - 1) as i:
                    body(i)
                body(PAIRS - 1, last=True)
                values(PAIRS - 1, 1)

            @block.vector
            def _(dve):
                def clip(n, hp):
                    dve.wait_ge(z_done.h, n + 1)
                    for which in range(2):
                        nc.vector.tensor_scalar(part(rest[hp], which), scores(hp, which), EXP_MAX, None,
                                                ALU.min).then_inc(clipped.h, 1)

                def softplus(n, hp):
                    for which in range(2):
                        dve.wait_ge(ln_ready.h, 2 * n + which + 1)
                        nc.vector.tensor_tensor(part(rest[hp], which), part(rest[hp], which), scores(hp, which),
                                                ALU.max).then_inc(rest_ready.h, 1)

                def stage_qk(i, first=False):
                    if not first:
                        dve.wait_ge(z_done.h, 2 * i)
                    for hp in range(2):
                        rows = slice(HD * hp, HD * hp + HD)
                        nc.vector.tensor_scalar(qs[hp][rows, :].rearrange("p (o t) -> p o t", o=1),
                                                qkv[rows, ds(i, 1), :], HD ** -0.5, None, ALU.mult)
                    nc.vector.tensor_scalar(ks[:, 0:T].rearrange("p (o t) -> p o t", o=1), qkv[:, ds(KT + i, 1), :],
                                            1.0, None, ALU.mult).then_inc(qk_staged.h, 1)

                def stage_v(i, hp, first):
                    if not first:
                        dve.wait_ge(pv_done.h, 2 * i - 1 + hp)
                    nc.vector.tensor_scalar(vs[hp][:], vtok[:, :, ds(i * P + hp * HD, HD)], 1.0, None,
                                            ALU.mult).then_inc(v_staged.h, 1)

                def out_low(i):
                    dve.wait_ge(ohi_ready.h, i + 1)
                    nc.vector.tensor_tensor(k.x_lo[:, ds(i, 1), 0:META], out_meta.rearrange("p (o t) -> p o t", o=1),
                                            k.x_hi[:, ds(i, 1), 0:META].bitcast(F32), ALU.subtract)
                    nc.vector.tensor_tensor(k.x_lo[:, ds(i, 1), META:T], out_main.rearrange("p (o t) -> p o t", o=1),
                                            k.x_hi[:, ds(i, 1), META:T].bitcast(F32),
                                            ALU.subtract).then_inc(out_free.h, 1)

                def body(i, first=False, last=False):
                    clip(2 * i, 0)
                    softplus(2 * i, 0)
                    if not last:
                        stage_qk(i + 1)
                    stage_v(i, 0, first)
                    clip(2 * i + 1, 1)
                    softplus(2 * i + 1, 1)
                    stage_v(i, 1, first)
                    if not first:
                        out_low(i - 1)

                stage_qk(0, first=True)
                body(0, first=True)
                with dve.Fori(1, PAIRS - 1) as i:
                    body(i)
                body(PAIRS - 1, last=True)
                out_low(PAIRS - 1)

            @block.scalar
            def _(act):
                def log_rest(n, hp):
                    for which in range(2):
                        act.wait_ge(clipped.h, 2 * n + which + 1)
                        nc.scalar.activation(part(rest[hp], which), part(rest[hp], which), ACT.Exp).then_inc(exp_done.h, 1)
                    for which in range(2):
                        act.wait_ge(exp_done.h, 2 * n + which + 1)
                        nc.scalar.activation(part(rest[hp], which), part(rest[hp], which), ACT.Ln,
                                             bias=k.eps[:, 1:2]).then_inc(ln_ready.h, 1)

                def rest_high(n, hp, first=False):
                    if not first:
                        act.wait_ge(later_done.h, n)
                    for which in range(2):
                        act.wait_ge(rest_ready.h, 2 * n + which + 1)
                        nc.scalar.activation(part(rest_hi, which), part(rest[hp], which), ACT.Copy).then_inc(rhi_ready.h, 1)

                def attend(n, hp, first=False):
                    act.wait_ge(later_done.h, n + 1)
                    if not first:
                        act.wait_ge(pv_done.h, n - 1)
                    for which in range(2):
                        nc.scalar.activation(part(att[hp], which), scores(hp, which), ACT.Exp).then_inc(att_ready.h, 1)

                def out_high(i):
                    act.wait_ge(pv_done.h, 2 * i + 2)
                    nc.scalar.activation(k.x_hi[:, ds(i, 1), 0:META], out_meta.rearrange("p (o t) -> p o t", o=1), ACT.Copy)
                    nc.scalar.activation(k.x_hi[:, ds(i, 1), META:T], out_main.rearrange("p (o t) -> p o t", o=1),
                                         ACT.Copy).then_inc(ohi_ready.h, 1)

                def body(i, first=False, last=False):
                    log_rest(2 * i + 1, 1)
                    attend(2 * i, 0, first)
                    if not first:
                        out_high(i - 1)
                    rest_high(2 * i + 1, 1)
                    if not last:
                        log_rest(2 * i + 2, 0)
                    attend(2 * i + 1, 1, first)
                    if not last:
                        rest_high(2 * i + 2, 0)

                nc.scalar.preload_act_table_set("natural_log_exp_and_others")
                log_rest(0, 0)
                rest_high(0, 0, first=True)
                body(0, first=True)
                with act.Fori(1, PAIRS - 1) as i:
                    body(i)
                body(PAIRS - 1, last=True)
                out_high(PAIRS - 1)



def columns(w, rows, at):
    r0, n = rows
    view = w[r0 * P:(r0 + n) * P, :].rearrange("(t p) c -> p t c", p=P)
    return lambda i, j: view[:, :, ds(at(i, j) * P, P)]


def ffn_gemms(d, n, fresh=False):
    out = []
    for half in range(2):
        w_in, w_out = d['w_ffn_in'][n], d['w_ffn_out'][n]
        out.append(Gemm(columns(w_in, (0, KT), lambda i, j, half=half: j * FT + half * FHALF + i), KT, FHALF,
                        fresh=fresh and half == 0))
        out.append(Gemm(columns(w_out, (half * FHALF, FHALF), lambda i, j: 2 * i + j), FHALF, KT // 2))
    return out


def ffn_layer(k, n, stages, nxt):
    with ExitStack() as tmp:
        norm = Norm(k, tmp, vcol(k, 'ffn_norm', n))
        m_hi, m_lo = (tmp.enter_context(k.nc.sbuf_tensor(f"mid_{n}{p}", [P, FHALF, T], F32R)) for p in ('hi', 'lo'))
        mid = [tmp.enter_context(k.nc.sbuf_tensor(f"{p}{n}", [P, 2, HALF], F32)) for p in ('sig', 'prod')]
        for half in range(2):
            follow = (stages + [nxt])[2 * half + 1:2 * half + 3]
            ffn_in_stage(k, stages[2 * half], follow[0], mid, m_hi, m_lo, norm if half == 0 else None)
            residual_stage(k, stages[2 * half + 1], follow[1], m_hi, m_lo)


def build_program(nc, d, out):
    with ExitStack() as ctx:
        k = setup(nc, d, ctx)
        k.v_first = nc.dram_tensor("v_first", [P, KT, T], F32).ap()
        pair = lambda i, j: 2 * i + j
        g_qkv = Gemm(columns(d['w_qkv'][0], (0, KT), pair), KT, 3 * KT // 2)
        g_wo = Gemm(columns(d['w_o_attn'][0], (0, KT), pair), KT, KT // 2)
        g_ffn = [ffn_gemms(d, n, fresh=n == 1) for n in range(2)]
        lora = lora_gemms(d)
        with ExitStack() as era:
            operands(k, era, "a")
            load_tokens(k, g_qkv)
            with ExitStack() as tmp:
                qkv = tmp.enter_context(nc.sbuf_tensor("qkv", [P, 3 * KT, T], F32))
                with ExitStack() as first:
                    qkv_stage(k, g_qkv, g_wo, qkv, Norm(k, first, vcol(k, 'attn_norm')))
                attention_stage(k, qkv)
            residual_stage(k, g_wo, g_ffn[0][0])
            ffn_layer(k, 0, g_ffn[0], lora['w'])
        rwkv_layer(k, d, lora, g_ffn[1])
        with ExitStack() as era:
            operands(k, era, "d")
            ffn_layer(k, 1, g_ffn[1], None)
        final_stage(k, out)


C = 64
CHUNKS = -(-T // C)
TP = CHUNKS * C
PAD = TP - T
DECAY = -math.exp(-0.5)
LEVELS = 6
LORA = {'w': ('w1', 'w2', 64), 'a': ('a1', 'a2', 64), 'v': ('v1', 'v2', 32)}
G_HALF = 80
LN_SHIFT = 20


def lora_gemms(d):
    out = {}
    for n, (first, second, rank) in LORA.items():
        out[n] = Gemm(lambda i, j, first=first, second=second:
                      d[first][0].rearrange("(t p) l -> p t l", p=P) if j == 0 else
                      d[second][0].rearrange("l (m c) -> l m c", c=P), KT, 1, fresh=n == 'w')
    out['g1'] = Gemm(lambda i, j: d['g1'][0][:, j * G_HALF:(j + 1) * G_HALF].rearrange("(t p) l -> p t l", p=P), KT, 1)
    out['g2'] = Gemm(lambda i, j: d['g2'][0][j * G_HALF:(j + 1) * G_HALF, :].rearrange("l (m c) -> l m c", c=P), KT, 1,
                     fresh=True)
    for n, which in (('r', 0), ('k', 1), ('v_big', 2)):
        out[n] = Gemm(columns(d['w_rkv'][0, which], (0, KT), lambda i, j: 2 * i + j), KT, KT // 2,
                      fresh=n == 'v_big')
    out['wo'] = Gemm(columns(d['w_o_rwkv'][0], (0, KT), lambda i, j: 2 * i + j), KT, KT // 2)
    return out


def real(t, m):
    return t[:, ds(m, 1), PAD:TP].rearrange("p o (a b) -> p (o a) b", a=2)


def row(t, m, cols=slice(None)):
    return t[:, ds(m, 1), cols].rearrange("p o t -> p (o t)")


def shift_vector(k, dve, xn, tmp, mu, done=0):
    nb = len(tmp)
    with dve.Fori(0, KT // nb) as i:
        for q in range(nb):
            m = nb * i + q
            dve.wait_ge(k.xl_ready.h, k.xl_ready.n + done + m + 1 - nb)
            k.nc.vector.tensor_tensor(tmp[q][:], row(xn, m, slice(0, T)), row(xn, m, slice(1, T + 1)),
                                      ALU.subtract).then_inc(k.sh_step.h, 1)
            dve.wait_ge(k.sh_step.h, k.sh_step.n + done + m + 1)
            k.nc.vector.scalar_tensor_tensor(tmp[q][:], tmp[q][:], mu(m), row(xn, m, slice(1, T + 1)),
                                             ALU.mult, ALU.add).then_inc(k.xn_ready.h, 1)


def shift_scalar(k, act, tmp):
    nb = len(tmp)
    with act.Fori(0, KT // nb) as i:
        for q in range(nb):
            m = nb * i + q
            act.wait_ge(k.xn_ready.h, k.xn_ready.n + m + 1)
            k.nc.scalar.activation(row(k.x_hi, m), tmp[q][:], ACT.Copy).then_inc(k.xh_ready.h, 1)


def shift_gpsimd(k, pool, tmp):
    nb = len(tmp)
    with pool.Fori(0, KT // nb) as i:
        for q in range(nb):
            m = nb * i + q
            pool.wait_ge(k.xh_ready.h, k.xh_ready.n + m + 1)
            k.nc.gpsimd.tensor_tensor(row(k.x_lo, m), tmp[q][:], row(k.x_hi, m).bitcast(F32),
                                      ALU.subtract).then_inc(k.xl_ready.h, 1)


def shifted_row(k):
    return lambda pe, t: pe.wait_ge(k.xl_ready.h, k.xl_ready.n + t + 1)


def shift_done(k):
    for c in (k.xn_ready, k.xh_ready, k.xl_ready, k.sh_step):
        c.n += KT


def lora_block(k, loras, nxt, r, g_hid):
    nc = k.nc
    b = k.bodies
    last_of = len(loras) - 1
    copies = [(k.x_hi, k.x_lo) if n % 2 else r.spare for n in range(len(loras))]
    seconds = [sum(1 for q in loras[:n] if q.out is not None) for n in range(len(loras))]
    xn0, xh0, xl0 = k.xn_ready.n, k.xh_ready.n, k.xl_ready.n
    read0, hid0 = k.lora_read.n, k.hid_ready.n
    nb = len(r.tmp)
    gate = [n for n, q in enumerate(loras) if q.out is None][0]

    with nc.Block() as block:
        @block.sync
        def _(sp):
            for n in range(len(loras)):
                follow = loras[n + 1].g if n < last_of else nxt
                for j in range(2):
                    sp.wait_ge(k.lo_ready[j].h, b + n + 1)
                    load_unit(k, sp, j, follow.src(0, j), follow.kt)
                if n == gate:
                    for j in range(2):
                        sp.wait_ge(k.psum_free[j].h, b + n + 2)
                    sp.dma_start(g_hid, r.ghid[:]).then_inc(k.stored.h, 16)
            sp.wait_ge(k.stored.h, k.stored.n + 16)

        @block.tensor
        def _(pe):
            def product(n, q, j):
                rows_hi, rows_lo = copies[n]
                pe.wait_ge(k.lo_ready[j].h, b + n + 1)
                pe.wait_ge(k.psum_free[j].h, b + n + 1)
                for half in range(2):
                    cols = slice(half * HALF, half * HALF + HALF)
                    for t in range(KT):
                        if half == 0 and j == 0:
                            pe.wait_ge(k.xl_ready.h, xl0 + KT * n + t + 1)
                        for a, (w, x) in enumerate(((k.w_hi, rows_hi), (k.w_hi, rows_lo), (k.w_lo, rows_hi))):
                            last = nc.tensor.matmul(k.psg[:, 2 * j + half, 0:HALF], w[j][:, t, :], x[:, t, cols],
                                                    start=t == 0 and a == 0, stop=t == KT - 1 and a == 2)
                last.then_inc(k.unit_done[j].h, 1)

            for n, q in enumerate(loras):
                product(n, q, 0)
                if q.out is None:
                    product(n, q, 1)
                    continue
                pe.wait_ge(k.lo_ready[1].h, b + n + 1)
                pe.wait_ge(k.psum_free[1].h, b + n + 2)
                for m in range(KT):
                    if seconds[n] * KT + m >= 2:
                        pe.wait_ge(k.lora_read.h, read0 + seconds[n] * KT + m - 1)
                    for half in range(2):
                        cols = slice(half * HALF, half * HALF + HALF)
                        for a, (w, x) in enumerate(((k.w_hi, r.hid_hi), (k.w_hi, r.hid_lo), (k.w_lo, r.hid_hi))):
                            last = nc.tensor.matmul(k.psx[:, 2 * (m % 2) + half, 0:HALF], w[1][0:q.rank, m, :],
                                                    x[0:q.rank, cols], start=a == 0, stop=a == 2)
                    if m < KT - 1:
                        last.then_inc(k.lora_done.h, 1)
                    else:
                        last.then_inc(k.unit_done[1].h, 1)

        @block.scalar
        def _(act):
            def high(n, rows):
                if n > last_of:
                    return
                rows_hi, _ = copies[n]
                if n >= 2 and rows.start == 0:
                    for j in range(2 if n - 2 == gate else 1):
                        act.wait_ge(k.unit_done[j].h, b + n - 1)
                for m in rows:
                    act.wait_ge(k.xn_ready.h, xn0 + KT * n + m + 1)
                    nc.scalar.activation(rows_hi[:, m, :], r.tmp[m % nb][:], ACT.Copy).then_inc(k.xh_ready.h, 1)

            def split(n, j):
                if n == last_of and nxt.fresh:
                    return
                follow = loras[n + 1].g if n < last_of else nxt
                act.wait_ge(k.raw_loaded[j].h, 16 * (b + n + 2))
                act.wait_ge(k.unit_done[j].h, b + n + 1)
                split_hi(k, j, follow.kt)

            high(0, range(KT))
            for n, q in enumerate(loras):
                act.wait_ge(k.unit_done[0].h, b + n + 1)
                if q.out is None:
                    for j in range(2):
                        act.wait_ge(k.unit_done[j].h, b + n + 1)
                        nc.scalar.activation(r.ghid[:, j, :].rearrange("p (a b) -> p a b", a=2),
                                             k.psg[0:G_HALF, 2 * j:2 * j + 2, 0:HALF],
                                             ACT.Sigmoid).then_inc(k.psum_free[j].h, 1)
                        split(n, j)
                        high(n + 1, range(j * KT // 2, (j + 1) * KT // 2))
                    continue
                nc.scalar.activation(r.hid[0:q.rank, :].rearrange("p (a b) -> p a b", a=2),
                                     k.psg[0:q.rank, 0:2, 0:HALF], q.func).then_inc(k.psum_free[0].h, 1)
                act.wait_ge(k.psum_free[0].h, b + n + 2)
                nc.scalar.activation(r.hid_hi[0:q.rank, :], r.hid[0:q.rank, :], ACT.Copy).then_inc(k.hid_ready.h, 1)
                split(n, 0)
                for m in range(KT):
                    high(n + 1, range(m, m + 1))
                    if m < KT - 1:
                        act.wait_ge(k.lora_done.h, k.lora_done.n + seconds[n] * (KT - 1) + m + 1)
                    else:
                        act.wait_ge(k.unit_done[1].h, b + n + 1)
                    nc.scalar.activation(real(q.out, m), k.psx[:, 2 * (m % 2):2 * (m % 2) + 2, 0:HALF], ACT.Sigmoid,
                                         bias=q.bias(m)).then_inc(k.lora_read.h, 1)
                split(n, 1)

        @block.vector
        def _(dve):
            def shift(n, rows):
                if n > last_of:
                    return
                for m in rows:
                    tmp, now = r.tmp[m % nb], r.xn[:, m, 1:T + 1]
                    dve.wait_ge(k.xl_ready.h, xl0 + KT * n + m + 1 - nb)
                    nc.vector.tensor_tensor(tmp[:], r.xn[:, m, 0:T], now, ALU.subtract).then_inc(k.sh_step.h, 1)
                    dve.wait_ge(k.sh_step.h, k.sh_step.n + KT * n + m + 1)
                    nc.vector.scalar_tensor_tensor(tmp[:], tmp[:], loras[n].mu(m), now, ALU.mult,
                                                   ALU.add).then_inc(k.xn_ready.h, 1)

            def split(n, j):
                if n == last_of and nxt.fresh:
                    return
                follow = loras[n + 1].g if n < last_of else nxt
                dve.wait_ge(k.hi_ready[j].h, b + n + 2)
                split_lo(k, j, follow.kt)

            shift(0, range(KT))
            for n, q in enumerate(loras):
                shift(n + 1, range(2))
                if q.out is not None:
                    dve.wait_ge(k.hid_ready.h, hid0 + seconds[n] + 1)
                    nc.vector.tensor_tensor(r.hid_lo[0:q.rank, :], r.hid[0:q.rank, :],
                                            r.hid_hi[0:q.rank, :].bitcast(F32),
                                            ALU.subtract).then_inc(k.psum_free[1].h, 1)
                split(n, 0)
                if q.out is None:
                    shift(n + 1, range(2, KT // 2))
                    split(n, 1)
                    shift(n + 1, range(KT // 2, KT))
                    continue
                shift(n + 1, range(2, KT))
                if n == last_of:
                    for w in range(len(loras)):
                        if loras[w].scan:
                            dve.wait_ge(k.lora_read.h, read0 + (seconds[w] + 1) * KT)
                            for m in range(KT):
                                nc.vector.tensor_tensor_scan(loras[w].out[:, m, :], r.reset[:], loras[w].out[:, m, :],
                                                             0.0, ALU.mult, ALU.add)
                split(n, 1)

        @block.gpsimd
        def _(pool):
            for n in range(len(loras)):
                _, rows_lo = copies[n]
                with pool.Fori(0, KT // len(r.tmp)) as i:
                    for u in range(len(r.tmp)):
                        m = len(r.tmp) * i + u
                        pool.wait_ge(k.xh_ready.h, xh0 + KT * n + m + 1)
                        nc.gpsimd.tensor_tensor(row(rows_lo, m), r.tmp[u][:],
                                                row(copies[n][0], m).bitcast(F32),
                                                ALU.subtract).then_inc(k.xl_ready.h, 1)
    for c in (k.xn_ready, k.xh_ready, k.xl_ready, k.sh_step):
        c.n += KT * len(loras)
    made = sum(1 for q in loras if q.out is not None)
    k.lora_read.n += KT * made
    k.lora_done.n += (KT - 1) * made
    k.hid_ready.n += made
    k.stored.n += 16
    k.bodies += len(loras)


class Lora:

    def __init__(self, g, mu, rank, func, bias, out, scan=False):
        self.g, self.mu, self.rank, self.func, self.bias, self.out, self.scan = g, mu, rank, func, bias, out, scan


def chunk_masks(k, ch, pool):
    nc = k.nc
    fills = [(ch.incl, 1.0), (ch.strict, 1.0), (ch.level_t, 0.0), (ch.eye, 0.0)]
    fills += [(e, 0.0) for e in ch.level]
    for t, value in fills:
        nc.gpsimd.memset(t[:], value).then_inc(ch.mk.h, 1)
    n = len(fills)
    pool.wait_ge(ch.mk.h, n)
    nc.gpsimd.memset(ch.level_t[:].rearrange("p (g two) -> p g two", two=2)[:, :, 1], 1.0).then_inc(ch.mk.h, 1)
    for e, mask in enumerate(ch.level):
        view = mask[:].rearrange("p (g two w) -> p g two w", two=2, w=2 ** e)
        nc.gpsimd.memset(view[:, :, 0, :], 1.0).then_inc(ch.mk.h, 1)
    n += 1 + LEVELS
    pool.wait_ge(ch.mk.h, n)
    for hp in range(2):
        rows = slice(C * hp, C * hp + C)
        view = ch.level_t[rows, :].rearrange("p (g two) -> p g two", two=2)[:, :, 1]
        steps = [(ch.incl[rows, :], ALU.is_ge, 0.0, 0, [[1, C]], -1),
                 (ch.strict[rows, :], ALU.is_gt, 0.0, 0, [[1, C]], -1),
                 (ch.eye[rows, :], ALU.not_equal, 1.0, 0, [[1, C]], -1),
                 (view, ALU.is_equal, 0.0, 0, [[-2, C // 2]], 1)]
        for e, mask in enumerate(ch.level):
            w = 2 ** e
            view = mask[rows, :].rearrange("p (g two w) -> p g two w", two=2, w=w)[:, :, 0, :]
            steps.append((view, ALU.is_ge, 0.0, -w, [[-2 * w, C // (2 * w)], [0, w]], 1))
            steps.append((view, ALU.is_ge, 0.0, 2 * w - 1, [[2 * w, C // (2 * w)], [0, w]], -1))
        for view, op, fill, base, pattern, by in steps:
            nc.gpsimd.affine_select(out=view, in_=view, compare_op=op, fill=fill, base=base, pattern=pattern,
                                    channel_multiplier=by).then_inc(ch.mk.h, 1)
            n += 1
            pool.wait_ge(ch.mk.h, n)


def v_stage(k, g, nxt, r, mu):
    nc = k.nc
    b = k.bodies
    with nc.Block() as block:
        @block.sync
        def _(sp):
            sp.dma_start(r.kk_in[:, :, PAD:TP], k.v_first).then_inc(k.vf_loaded.h, 16)
            gemm_sync(k, sp, g, nxt)

        @block.gpsimd
        def _(pool):
            shift_gpsimd(k, pool, r.tmp)
            for t in (r.vv, r.kk_in):
                nc.gpsimd.memset(t[:, :, 0:PAD], 0.0)
            chunk_masks(k, r.ch, pool)

        @block.tensor
        def _(pe):
            gemm_tensor(k, pe, g, row_ready=shifted_row(k))

        @block.scalar
        def _(act):
            for j in range(2):
                act.wait_ge(k.raw_loaded[j].h, 16 * (b + 1))
                split_hi(k, j, g.kt)
            shift_scalar(k, act, r.tmp)
            gemm_scalar(k, act, g, nxt, lambda i, j: None)

        @block.vector
        def _(dve):
            for j in range(2):
                dve.wait_ge(k.hi_ready[j].h, b + 1)
                split_lo(k, j, g.kt)
            shift_vector(k, dve, r.xn, r.tmp, mu)
            dve.wait_ge(k.vf_loaded.h, 16)

            def epilogue(i, j):
                m = 2 * i + j
                n = k.v_step.n + 2 * m
                dve.wait_ge(k.unit_done[j].h, b + i + 1)
                nc.vector.tensor_tensor(real(r.vv, m), real(r.kk_in, m), halves(k, j), ALU.subtract).then_inc(k.v_step.h, 1)
                dve.wait_ge(k.v_step.h, n + 1)
                nc.vector.tensor_tensor(real(r.vv, m), real(r.vv, m), real(r.rr, m), ALU.mult).then_inc(k.v_step.h, 1)
                dve.wait_ge(k.v_step.h, n + 2)
                nc.vector.tensor_tensor(real(r.vv, m), real(r.vv, m), halves(k, j), ALU.add).then_inc(k.psum_free[j].h, 1)
            gemm_vector(k, dve, g, nxt, epilogue)
    shift_done(k)
    k.v_step.n += 2 * KT
    k.bodies += g.bodies


def k_stage(k, g, nxt, r, mu):
    nc = k.nc
    b = k.bodies
    with nc.Block() as block:
        @block.sync
        def _(sp):
            gemm_sync(k, sp, g, nxt)

        @block.tensor
        def _(pe):
            gemm_tensor(k, pe, g, row_ready=shifted_row(k))

        @block.scalar
        def _(act):
            shift_scalar(k, act, r.tmp)

            def epilogue(i, j):
                act.wait_ge(k.unit_done[j].h, b + i + 1)
                nc.scalar.activation(real(r.kk_in, 2 * i + j), halves(k, j), ACT.Copy).then_inc(k.psum_free[j].h, 1)
            gemm_scalar(k, act, g, nxt, epilogue)

        @block.vector
        def _(dve):
            shift_vector(k, dve, r.xn, r.tmp, mu)
            gemm_vector(k, dve, g, nxt, lambda i, j: None)

        @block.gpsimd
        def _(pool):
            shift_gpsimd(k, pool, r.tmp)
    shift_done(k)
    k.bodies += g.bodies


def r_stage(k, g, nxt, r, mu):
    nc = k.nc
    b = k.bodies
    half_tp = TP // 2
    kkc, kac = vcol(k, 'k_k'), vcol(k, 'k_a')
    with nc.Block() as block:
        @block.sync
        def _(sp):
            gemm_sync(k, sp, g, nxt)

        @block.tensor
        def _(pe):
            def head_sums(i, j):
                m = 2 * i + j
                pe.wait_ge(k.sq_ready.h, k.sq_ready.n + m + 1)
                pe.wait_ge(k.kn_clip.h, k.kn_clip.n + m)
                for half in range(2):
                    last = nc.tensor.matmul(k.psx[:, half, 0:half_tp], r.heads[:],
                                            r.sq[:, half * half_tp:(half + 1) * half_tp], start=True, stop=True)
                last.then_inc(k.kn_sum.h, 1)
            gemm_tensor(k, pe, g, extra=head_sums, row_ready=shifted_row(k))

        @block.scalar
        def _(act):
            shift_scalar(k, act, r.tmp)

            def square(i, j):
                m = 2 * i + j
                act.wait_ge(k.kn_raw.h, k.kn_raw.n + m + 1)
                act.wait_ge(k.kn_sum.h, k.kn_sum.n + m)
                nc.scalar.activation(r.sq[:], row(r.xn, m), ACT.Square).then_inc(k.sq_ready.h, 1)

            def epilogue(i, j):
                m = 2 * i + j
                act.wait_ge(k.unit_done[j].h, b + i + 1)
                nc.scalar.activation(real(r.rr, m), halves(k, j), ACT.Copy).then_inc(k.psum_free[j].h, 1)
                act.wait_ge(k.kn_clip.h, k.kn_clip.n + m + 1)
                nc.scalar.activation(r.norm[:], r.norm[:], ACT.Ln, scale=2.0 ** LN_SHIFT).then_inc(k.kn_ln.h, 1)
                act.wait_ge(k.kn_ln.h, k.kn_ln.n + m + 1)
                nc.scalar.activation(r.norm[:], r.norm[:], ACT.Exp, scale=-0.5, bias=r.cst[:, 0:1]).then_inc(k.kn_exp.h, 1)
            gemm_scalar(k, act, g, nxt, epilogue, before=square, split_first=True)

        @block.vector
        def _(dve):
            shift_vector(k, dve, r.xn, r.tmp, mu)
            dve.wait_ge(k.xl_ready.h, k.xl_ready.n + KT)

            def raw_kk(i, j):
                m = 2 * i + j
                nc.vector.tensor_scalar(row(r.xn, m), row(r.kk_in, m), kkc(m), None, ALU.mult).then_inc(k.kn_raw.h, 1)

            def epilogue(i, j):
                m = 2 * i + j
                dve.wait_ge(k.kn_sum.h, k.kn_sum.n + m + 1)
                dve.wait_ge(k.kn_used.h, k.kn_used.n + m)
                nc.vector.tensor_scalar(r.norm[:].rearrange("p (a b) -> p a b", a=2), k.psx[:, 0:2, 0:half_tp],
                                        1e-24, None, ALU.max).then_inc(k.kn_clip.h, 1)
                nc.vector.tensor_scalar(r.ka[:], row(r.aa, m), kac(m), r.omka[:, ds(m, 1)], ALU.mult,
                                        ALU.add).then_inc(k.ka_step.h, 1)
                dve.wait_ge(k.ka_step.h, k.ka_step.n + m + 1)
                nc.vector.tensor_tensor(row(r.kk_in, m), row(r.kk_in, m), r.ka[:], ALU.mult)
                dve.wait_ge(k.kn_exp.h, k.kn_exp.n + m + 1)
                nc.vector.tensor_tensor(row(r.xn, m), row(r.xn, m), r.norm[:], ALU.mult).then_inc(k.kn_used.h, 1)
                dve.wait_ge(k.kn_used.h, k.kn_used.n + m + 1)
                nc.vector.tensor_tensor(row(r.aa, m), row(r.aa, m), row(r.xn, m), ALU.mult).then_inc(k.b_ready.h, 1)
            gemm_vector(k, dve, g, nxt, epilogue, before=raw_kk, split_first=True)

        @block.gpsimd
        def _(pool):
            shift_gpsimd(k, pool, r.tmp)
    shift_done(k)
    for c in (k.sq_ready, k.kn_clip, k.kn_sum, k.kn_raw, k.kn_ln, k.kn_exp, k.kn_used, k.ka_step):
        c.n += KT
    k.bodies += g.bodies


def chunk_stage(k, r):
    nc = k.nc
    with ExitStack() as tmp:
        def sb(name, shape, dt=F32):
            return tmp.enter_context(nc.sbuf_tensor(name, shape, dt))

        ch = r.ch
        ch.w_ext, ch.w_inv = sb("w_ext", [P, KT, C + 1]), sb("w_inv", [P, KT, C])
        ch.state = sb("state", [P, KT, C])
        ar, bkt = ([sb(f"{n}{q}", [P, KT, 2, C]) for q in range(2)] for n in ("ar", "bkt"))
        uv, arm = ([sb(f"{n}{q}", [P, H, C]) for q in range(2)] for n in ("uv", "arm"))
        xt, av = ([sb(f"{n}{q}", [P, KT, C]) for q in range(2)] for n in ("xt", "av"))
        w_end = [sb(f"w_end{q}", [P, KT, 1]) for q in range(2)]
        bk, akm = sb("bk", [P, KT, 2, C]), sb("akm", [P, H, C])
        low, xs, tt, wt, vc = (sb(n, [P, KT, C]) for n in ("low", "xs", "tt", "wt", "vc"))
        half_unit = KT * C // P
        es = [k.raw[n // 2][:, (n % 2) * half_unit:(n % 2 + 1) * half_unit, :].rearrange("p a (b c) -> p (a b) c", c=C)
              for n in range(4)] + [sb("es4", [P, KT, C])]
        (exps, vc_r, wend_r, ar_r, bk_r, lps, low_r, tb_d, bkt_r, tv_d, uvv_r, quad, arm_r, av_d, av_r, e_r, xt_r, xs_r,
         x_step, t_d, t_r, dx_d, w_d, wt_r, u_d, u_r, y_d, y_r, s_d, s_step, state_r, settled, ones_r) = (
            k.sem("c_" + n) for n in (
                "exps", "vcopied", "w_end", "ar", "bk", "lproduct", "low", "bk_turned", "bkt", "v_turned", "uv_v", "quad",
                "arm", "av_done", "av", "e", "xt", "xs", "x_step", "t_done", "t", "dx", "w_done", "w", "u_done", "u",
                "y_done", "y", "s_done", "s_step", "state", "settled", "first_set"))
        bank = [k.psg[:, n, :].rearrange("p (m c) -> p m c", c=C) for n in range(4)]
        bank += [k.psx[:, n, :].rearrange("p (m c) -> p m c", c=C) for n in range(4)]
        lt_ps, l_ps, t_ps, wy_ps, s_ps = bank[0], bank[1], bank[2], bank[3], bank[6]
        pair_ps, u_ps = k.psx[:, 0:2, :], k.psx[:, 2:4, :]
        heads = [(h, h // 2, slice(HD * (h % 2), HD * (h % 2) + HD)) for h in range(H)]

        levels = LEVELS - 1
        first_levels = (META - 1).bit_length() - 1

        def levels_of(n):
            return first_levels if type(n) is int and n == 0 else levels

        def level_count(n, e):
            return e + 1 if type(n) is int and n == 0 else levels * n + (first_levels - levels + e + 1)

        def xt_count(n, j):
            return j + 1 if type(n) is int and n == 0 else (levels + 1) * n + (first_levels - levels + j + 1)

        def xs_count(n, j):
            return j + 1 if type(n) is int and n == 0 else levels * n + (first_levels - levels + j + 1)

        def at(h):
            return (h % 2) * KT + h // 2

        def over_rows(mask):
            return mask[:].rearrange("p (o c) -> p o c", o=1).broadcast_to([P, KT, C])

        def chunk(t, c):
            return t[:, :, ds(c * C, C)]

        def steps(eng, step):
            step(-1, 1, False, True, True)
            step(0, 0, True, True, True)
            with eng.Fori(0, (CHUNKS - 3) // 2) as i:
                step(2 * i + 1, 1, True, True, True)
                step(2 * i + 2, 0, True, True, True)
            step(CHUNKS - 2, (CHUNKS - 2) % 2, True, True, False)
            step(CHUNKS - 1, (CHUNKS - 1) % 2, True, False, False)

        with nc.Block() as block:
            @block.scalar
            def _(act):
                def decays(n):
                    nc.scalar.activation(ch.w_ext[:, :, 1:C + 1], chunk(r.gs, n), ACT.Exp, scale=DECAY)
                    nc.scalar.activation(ch.w_inv[:], chunk(r.gs, n), ACT.Exp, scale=-DECAY).then_inc(exps.h, 1)

                def copy_v(n):
                    nc.scalar.activation(vc[:], chunk(r.vv, n), ACT.Copy).then_inc(vc_r.h, 1)

                def copy_t(n, e):
                    act.wait_ge(t_d.h, level_count(n, e))
                    cols = slice(C // 2 if e == levels - 1 else 0, C)
                    nc.scalar.activation(tt[:, :, cols], t_ps[:, :, cols], ACT.Copy).then_inc(t_r.h, 1)

                def step(c, q, chain, prep, ahead):
                    n, p = c + 1, 1 - q
                    if prep:
                        act.wait_ge(lps.h, n + 1)
                        nc.scalar.activation(low[:], l_ps, ACT.Copy).then_inc(low_r.h, 1)
                        act.wait_ge(tb_d.h, n + 1)
                        nc.scalar.activation(bkt[p][:].rearrange("p m a c -> p (m a) c"),
                                             pair_ps.rearrange("p b (m c) -> p (b m) c", c=C),
                                             ACT.Copy).then_inc(bkt_r.h, 1)
                        copy_t(n, 0)
                    if chain:
                        act.wait_ge(u_d.h, c + 1)
                        nc.scalar.activation(uv[q][0:C, :, :], u_ps[0:C].rearrange("p b (m c) -> p (b m) c", c=C),
                                             ACT.Copy).then_inc(u_r.h, 1)
                    if prep:
                        copy_t(n, 1)
                        if not (type(c) is int and c <= 0):
                            act.wait_ge(state_r.h, c)
                        nc.scalar.activation(w_end[p][:], r.gs[:, :, ds(n * C + C - 1, 1)], ACT.Exp,
                                             scale=DECAY).then_inc(wend_r.h, 1)
                        copy_t(n, 2)
                        if ahead:
                            decays(n + 1)
                            copy_v(n + 1)
                        for e in range(3, levels_of(n)):
                            copy_t(n, e)
                        act.wait_ge(av_d.h, n + 1)
                        nc.scalar.activation(av[p][:], l_ps, ACT.Copy).then_inc(av_r.h, 1)

                decays(0)
                copy_v(0)
                steps(act, step)

            @block.gpsimd
            def _(pool):
                def products(n):
                    pool.wait_ge(exps.h, n + 1)
                    if not (type(n) is int and n == 0):
                        pool.wait_ge(quad.h, 2 * n)
                    nc.gpsimd.tensor_tensor(bk[:, :, 0, :], chunk(r.aa, n), ch.w_inv[:], ALU.mult)
                    nc.gpsimd.tensor_tensor(bk[:, :, 1, :], chunk(r.kk_in, n), ch.w_inv[:], ALU.mult).then_inc(bk_r.h, 1)

                def step(c, q, chain, prep, ahead):
                    n = c + 1
                    if prep:
                        pool.wait_ge(low_r.h, n + 1)
                        for e in range(levels_of(n)):
                            nc.gpsimd.tensor_tensor(es[e][:], low[:], over_rows(ch.level[e + 1]),
                                                    ALU.mult).then_inc(e_r.h, 1)
                    if ahead:
                        products(n + 1)

                products(0)
                steps(pool, step)

            @block.vector
            def _(dve):
                def products(n, p):
                    dve.wait_ge(exps.h, n + 1)
                    if type(n) is int and n == 0:
                        nc.vector.memset(ch.w_ext[:, :, 0:1], 1.0).then_inc(ones_r.h, 1)
                        nc.vector.memset(ch.state[:], 0.0).then_inc(ones_r.h, 1)
                        dve.wait_ge(ones_r.h, 2)
                    nc.vector.tensor_tensor(ar[p][:, :, 0, :], chunk(r.xn, n), ch.w_ext[:, :, 0:C], ALU.mult)
                    nc.vector.tensor_tensor(ar[p][:, :, 1, :], chunk(r.rr, n), ch.w_ext[:, :, 1:C + 1],
                                            ALU.mult).then_inc(ar_r.h, 1)

                def first_xt(n, p):
                    dve.wait_ge(lps.h, n + 1)
                    nc.vector.scalar_tensor_tensor(xt[p][:], lt_ps, -1.0, over_rows(ch.level_t), ALU.mult, ALU.mult)\
                        .then_inc(x_step.h, 1)
                    dve.wait_ge(x_step.h, 2 * n + 1)
                    nc.vector.tensor_tensor(xt[p][:], xt[p][:], over_rows(ch.eye), ALU.add).then_inc(xt_r.h, 1)

                def first_xs(n):
                    dve.wait_ge(low_r.h, n + 1)
                    nc.vector.scalar_tensor_tensor(xs[:], low[:], -1.0, over_rows(ch.level[0]), ALU.mult, ALU.mult)\
                        .then_inc(x_step.h, 1)
                    dve.wait_ge(x_step.h, 2 * n + 2)
                    nc.vector.tensor_tensor(xs[:], xs[:], over_rows(ch.eye), ALU.add).then_inc(xs_r.h, 1)

                def next_x(n, p, e):
                    dve.wait_ge(dx_d.h, level_count(n, e))
                    if e == levels - 1:
                        for rows in (slice(0, C // 2), slice(C, C + C // 2)):
                            quarter = xt[p][rows, :, C // 2:C]
                            last = nc.vector.tensor_tensor(quarter, quarter, lt_ps[rows, :, C // 2:C], ALU.subtract)
                        last.then_inc(xt_r.h, 1)
                    else:
                        nc.vector.tensor_tensor(xt[p][:], xt[p][:], lt_ps, ALU.subtract).then_inc(xt_r.h, 1)
                    if e == levels - 2:
                        for rows in (slice(0, C // 2), slice(C, C + C // 2)):
                            quarter = xs[rows, :, 0:C // 2]
                            last = nc.vector.tensor_tensor(quarter, quarter, l_ps[rows, :, 0:C // 2], ALU.subtract)
                        last.then_inc(xs_r.h, 1)
                    elif e < levels_of(n) - 1:
                        nc.vector.tensor_tensor(xs[:], xs[:], l_ps, ALU.subtract).then_inc(xs_r.h, 1)

                def quads(n, p, half):
                    dve.wait_ge(quad.h, 2 * n + half + 1)
                    quad_ps = pair_ps.rearrange("p b (m c) -> p b m c", c=2 * C)
                    ms = slice(half * KT // 2, (half + 1) * KT // 2)
                    def masks(mask):
                        rows, _ = mask.shape
                        return mask.rearrange("p (o a c) -> p o a c", o=1, a=1).broadcast_to([rows, 2, KT // 2, C])
                    nc.vector.tensor_tensor(akm[C:P, :, :].rearrange("p (b m) c -> p b m c", b=2)[:, :, ms, :],
                                            quad_ps[C:P, :, :, 0:C], masks(ch.strict[C:P, :]), ALU.mult)
                    nc.vector.tensor_tensor(arm[p][:].rearrange("p (b m) c -> p b m c", b=2)[:, :, ms, :],
                                            quad_ps[:, :, :, C:2 * C], masks(ch.incl[:]), ALU.mult).then_inc(arm_r.h, 1)

                def step(c, q, chain, prep, ahead):
                    n, p = c + 1, 1 - q
                    if prep:
                        first_xt(n, p)
                    if chain:
                        dve.wait_ge(av_r.h, c + 1)
                        dve.wait_ge(w_d.h, c + 1)
                        nc.vector.scalar_tensor_tensor(wt[:], wy_ps, -1.0, av[q][:], ALU.mult, ALU.subtract)\
                            .then_inc(wt_r.h, 1)
                    if prep:
                        first_xs(n)
                        next_x(n, p, 0)
                        dve.wait_ge(tv_d.h, n + 1)
                        nc.vector.tensor_copy(uv[p][C:P, :, :].rearrange("p (two m) c -> p m two c", two=2),
                                              pair_ps[C:P].rearrange("p b (m two c) -> p (b m) two c", two=2, c=C))\
                            .then_inc(uvv_r.h, 1)
                        next_x(n, p, 1)
                        quads(n, p, 0)
                    if chain:
                        dve.wait_ge(y_d.h, c + 1)
                        nc.vector.tensor_scalar(chunk(r.xn, c), wy_ps, 1.0, None, ALU.mult).then_inc(y_r.h, 1)
                    if prep:
                        if levels_of(n) == 3:
                            quads(n, p, 1)
                        next_x(n, p, 2)
                        if levels_of(n) > 3:
                            quads(n, p, 1)
                        for e in range(3, levels_of(n) - 1):
                            next_x(n, p, e)
                        if ahead:
                            products(n + 1, q)
                        if levels_of(n) > 3:
                            next_x(n, p, levels_of(n) - 1)
                    if chain and prep:
                        dve.wait_ge(s_d.h, c + 1)
                        nc.vector.tensor_tensor(ch.state[:], ch.state[:], s_ps, ALU.add).then_inc(s_step.h, 1)
                        dve.wait_ge(s_step.h, c + 1)
                        dve.wait_ge(wend_r.h, c + 1)
                        nc.vector.tensor_tensor(ch.state[:], ch.state[:], w_end[q][:].broadcast_to([P, KT, C]),
                                                ALU.mult).then_inc(state_r.h, 1)

                products(0, 0)
                steps(dve, step)

            @block.tensor
            def _(pe):
                mm = nc.tensor.matmul

                def settle():
                    pe.sem_inc(settled.h, 1)

                def l_products(n, p):
                    pe.wait_ge(ar_r.h, n + 1)
                    pe.wait_ge(bk_r.h, n + 1)
                    if not (type(n) is int and n == 0):
                        pe.wait_ge(xt_r.h, xt_count(n - 1, levels_of(n - 1)))
                        pe.wait_ge(av_r.h, n)
                    settle()
                    for h, m, rows in heads:
                        mm(lt_ps[rows, m, :], bk[rows, m, 0, :], ar[p][rows, m, 0, :], start=True, stop=True)
                    for h, m, rows in heads:
                        last = mm(l_ps[rows, m, :], ar[p][rows, m, 0, :], bk[rows, m, 0, :], start=True, stop=True)
                    last.then_inc(lps.h, 1)

                def turn_bk(n):
                    if not (type(n) is int and n == 0):
                        pe.wait_ge(arm_r.h, 2 * n)
                    for m in range(KT):
                        last = nc.tensor.transpose(pair_ps[:, m // 4, (m % 4) * P:(m % 4) * P + P],
                                                   bk[:, m, :, :].rearrange("p a c -> p (a c)"), k.ident[:])
                    last.then_inc(tb_d.h, 1)

                def turn_v(n):
                    pe.wait_ge(vc_r.h, n + 1)
                    pe.wait_ge(bkt_r.h, n + 1)
                    settle()
                    for m in range(KT):
                        last = mm(pair_ps[C:P, m // 4, (m % 4) * P:(m % 4) * P + P], vc[:, m, :], k.ident[:],
                                  start=True, stop=True)
                    last.then_inc(tv_d.h, 1)

                def quads(n, p, half, parts=(0, 1)):
                    if half == 0:
                        pe.wait_ge(uvv_r.h, n + 1)
                    elif parts[0] == 0:
                        pe.wait_ge(arm_r.h, 2 * n + 1)
                    first = half * KT + parts[0] * KT // 2
                    for h, m, rows in heads[first:first + len(parts) * KT // 2]:
                        last = mm(pair_ps[:, h % 2, (m % 4) * P:(m % 4) * P + P],
                                  bk[rows, m, :, :].rearrange("p a c -> p (a c)"),
                                  ar[p][rows, m, :, :].rearrange("p a c -> p (a c)"), start=True, stop=True)
                    if parts[-1] == 1:
                        last.then_inc(quad.h, 1)

                def a_v(n, p):
                    pe.wait_ge(arm_r.h, 2 * n + 2)
                    pe.wait_ge(xs_r.h, xs_count(n, levels_of(n) - 1))
                    settle()
                    for h, m, rows in heads:
                        last = mm(l_ps[rows, m, :], akm[C:P, at(h), :], uv[p][C:P, at(h), :], start=True, stop=True)
                    last.then_inc(av_d.h, 1)

                def times_x(n, p, e):
                    pe.wait_ge(xt_r.h, xt_count(n, e))
                    pe.wait_ge(e_r.h, level_count(n, e))
                    settle()
                    for h, m, rows in heads:
                        if e == levels - 1:
                            low_rows = slice(rows.start, rows.start + C // 2)
                            last = mm(t_ps[low_rows, m, C // 2:C], es[e][rows, m, 0:C // 2], xt[p][rows, m, C // 2:C],
                                      start=True, stop=True)
                        else:
                            last = mm(t_ps[rows, m, :], es[e][rows, m, :], xt[p][rows, m, :], start=True, stop=True)
                    last.then_inc(t_d.h, 1)

                def x_times(n, e):
                    pe.wait_ge(t_r.h, level_count(n, e))
                    pe.wait_ge(xs_r.h, xs_count(n, e))
                    settle()
                    for h, m, rows in heads:
                        if e == levels - 1:
                            low_rows = slice(rows.start, rows.start + C // 2)
                            last = mm(lt_ps[low_rows, m, C // 2:C], xs[low_rows, m, 0:C // 2], tt[low_rows, m, C // 2:C],
                                      start=True, stop=True)
                        else:
                            last = mm(lt_ps[rows, m, :], xs[rows, m, :], tt[rows, m, :], start=True, stop=True)
                    if e < levels_of(n) - 1:
                        for h, m, rows in heads:
                            if e == levels - 2:
                                rows = slice(rows.start, rows.start + C // 2)
                                last = mm(l_ps[rows, m, 0:C // 2], tt[rows, m, 0:C // 2], xs[rows, m, 0:C // 2],
                                          start=True, stop=True)
                            else:
                                last = mm(l_ps[rows, m, :], tt[rows, m, :], xs[rows, m, :], start=True, stop=True)
                    last.then_inc(dx_d.h, 1)

                def chain_w(c, q):
                    if not (type(c) is int and c == 0):
                        pe.wait_ge(state_r.h, c)
                        pe.wait_ge(y_r.h, c)
                        settle()
                    for h, m, rows in heads:
                        last = mm(wy_ps[rows, m, :], ar[q][rows, m, 0, :], ch.state[rows, m, :], start=True, stop=True)
                    last.then_inc(w_d.h, 1)

                def chain_u(c, q):
                    pe.wait_ge(wt_r.h, c + 1)
                    settle()
                    for h, m, rows in heads:
                        last = mm(u_ps[0:C, h % 2, m * C:m * C + C], xt[q][rows, m, :], wt[rows, m, :], start=True,
                                  stop=True)
                    last.then_inc(u_d.h, 1)

                def chain_y_state(c, q):
                    for h, m, rows in heads:
                        mm(wy_ps[rows, m, :], ch.state[rows, m, :], ar[q][rows, m, 1, :], start=m == 0, stop=True,
                           skip_group_check=True)

                def chain_y(c, q):
                    pe.wait_ge(u_r.h, c + 1)
                    for h, m, rows in heads:
                        last = mm(wy_ps[rows, m, :], uv[q][:, at(h), :], arm[q][:, at(h), :], start=False, stop=True,
                                  skip_group_check=True)
                    last.then_inc(y_d.h, 1)

                def chain_s(c, q):
                    for h, m, rows in heads:
                        last = mm(s_ps[rows, m, :], bkt[q][:].rearrange("p m a c -> p m (a c)")[:, m, rows],
                                  uv[q][:, at(h), :], start=True, stop=True)
                    last.then_inc(s_d.h, 1)

                def step(c, q, chain, prep, ahead):
                    n, p = c + 1, 1 - q
                    if prep:
                        l_products(n, p)
                    if chain:
                        chain_w(c, q)
                    if prep:
                        turn_bk(n)
                        times_x(n, p, 0)
                    if chain:
                        chain_u(c, q)
                    if prep:
                        x_times(n, 0)
                        turn_v(n)
                        times_x(n, p, 1)
                    if chain:
                        chain_y_state(c, q)
                    if prep:
                        x_times(n, 1)
                        quads(n, p, 0)
                        times_x(n, p, 2)
                    if chain:
                        chain_y(c, q)
                    if prep:
                        if levels_of(n) == 3:
                            quads(n, p, 1)
                            a_v(n, p)
                            x_times(n, 2)
                        else:
                            x_times(n, 2)
                            quads(n, p, 1, (0,))
                            times_x(n, p, 3)
                            quads(n, p, 1, (1,))
                            x_times(n, 3)
                            times_x(n, p, 4)
                            a_v(n, p)
                            x_times(n, 4)
                    if chain and prep:
                        chain_s(c, q)

                steps(pe, step)


def rwkv_layer(k, d, lora, g_ffn):
    nc = k.nc
    g_hid = nc.dram_tensor("g_hid", [G_HALF, 2, T], F32).ap()
    names = ('r', 'k', 'v', 'w', 'a', 'g')
    mus = {n: vcol(k, 'mu', i) for i, n in enumerate(names)}
    r = State()
    with ExitStack() as arrays:
        def sb(name, shape, dt=F32, where=arrays):
            return where.enter_context(nc.sbuf_tensor(name, shape, dt))
        r.heads = sb("heads", [P, P])
        r.ch = State()
        r.ch.mk = k.sem("chunk_masks")
        r.ch.incl, r.ch.strict, r.ch.level_t, r.ch.eye = (sb(n, [P, C]) for n in ("incl", "strict", "level_t", "eye"))
        r.ch.level = [sb(f"level{e}", [P, C]) for e in range(LEVELS)]
        r.cst, r.omka = sb("cst_ln", [P, 1]), sb("omka", [P, KT])
        r.gs, r.aa, r.rr, r.xn = (sb(n, [P, KT, TP]) for n in ("gs", "aa", "rr", "xn"))
        with ExitStack() as era:
            r.spare = [sb(f"spare_{n}", [P, KT, T], F32R, era) for n in ("hi", "lo")]
            operands(k, era, "b")
            r.tmp = [sb(f"shifted{q}", [P, T], where=era) for q in range(SHIFT_BUFFERS)]
            r.hid = sb("hid", [C, T], where=era)
            r.hid_hi, r.hid_lo = (sb(n, [C, T], F32R, where=era) for n in ("hid_hi", "hid_lo"))
            r.reset = sb("reset", [P, TP], where=era)
            r.ghid = sb("ghid", [G_HALF, 2, T], where=era)
            rwkv_norm(k, r, vcol(k, 'rwkv_norm'), lora['w'])
            loras = [Lora(lora['w'], mus['w'], 64, ACT.Tanh, vcol(k, 'w0'), r.gs, True),
                     Lora(lora['a'], mus['a'], 64, ACT.Copy, vcol(k, 'a0'), r.aa),
                     Lora(lora['g1'], mus['g'], 2 * G_HALF, ACT.Sigmoid, None, None),
                     Lora(lora['v'], mus['v'], 32, ACT.Copy, vcol(k, 'v0'), r.rr)]
            lora_block(k, loras, lora['v_big'], r, g_hid)
        r.vv, r.kk_in = (sb(n, [P, KT, TP]) for n in ("vv", "kk_in"))
        with ExitStack() as era:
            operands(k, era, "e")
            r.tmp = [sb(f"shifted_e{q}", [P, T], where=era) for q in range(SHIFT_BUFFERS)]
            r.sq, r.norm, r.ka = (sb(n, [P, TP], where=era) for n in ("kk_sq", "norm", "ka"))
            v_stage(k, lora['v_big'], lora['k'], r, mus['v'])
            k_stage(k, lora['k'], lora['r'], r, mus['k'])
            r_stage(k, lora['r'], None, r, mus['r'])
        chunk_stage(k, r)
        with ExitStack() as era:
            operands(k, era, "c")
            output_stage(k, lora['g2'], lora['wo'], r, g_hid)
            begin_at(k, META)
            residual_stage(k, lora['wo'], g_ffn[0])


def rwkv_norm(k, r, gain, first):
    nc = k.nc
    with nc.Block() as block:
        @block.scalar
        def _(act):
            norm_scalar(k, act, r.rr[:, :, PAD:TP], split=False, fresh=first)

        @block.tensor
        def _(pe):
            norm_tensor(k, pe, r.rr[:, :, PAD:TP])

        @block.vector
        def _(dve):
            norm_vector(k, dve, r.rr[:, :, PAD:TP], lambda m: r.xn[:, ds(m, 1), 1:T + 1], gain, first)

        @block.gpsimd
        def _(pool):
            nc.gpsimd.memset(r.xn[:, :, 0:1], 0.0)
            nc.gpsimd.memset(r.heads[:], 0.0).then_inc(k.pads.h, 1)
            nc.gpsimd.memset(r.reset[:], 1.0).then_inc(k.pads.h, 1)
            nc.gpsimd.memset(r.cst[:], 0.5 * LN_SHIFT * math.log(2.0))
            for t in (r.gs, r.aa, r.rr):
                nc.gpsimd.memset(t[:, :, 0:PAD], 0.0)
            pool.wait_ge(k.pads.h, 2)
            nc.gpsimd.memset(r.reset[:].rearrange("p (c t) -> p c t", t=C)[:, :, 0:1], 0.0)
            nc.gpsimd.memset(r.heads[0:HD, 0:HD], 1.0)
            n = VECTORS.index(('k_a', 0))
            nc.gpsimd.tensor_scalar(r.omka[:], k.vec[:, n, :], -1.0, 1.0, ALU.mult, ALU.add).then_inc(k.pads.h, 1)
            pool.wait_ge(k.pads.h, 3)
            nc.gpsimd.memset(r.heads[HD:P, HD:P], 1.0).then_inc(k.pads.h, 1)
            pool.wait_ge(k.pads.h, 4)
    for c in (k.sq_ready, k.xn_ready):
        c.n += KT
    k.pair_ready.n += KT // 2
    k.sum_ready.n += 1
    k.rs_step.n += 2


def output_stage(k, g, nxt, r, g_hid):
    nc = k.nc
    b = k.bodies
    y = r.xn
    prod, cent, sq, rs = ([r.gs[:, 2 * n + q, 0:SEQ] for q in range(2)] for n in range(4))
    bon, fin = ([r.aa[:, 2 * n + q, 0:SEQ] for q in range(2)] for n in (1, 2))
    ps = [k.psx, k.psg]
    BONUS, MEAN, VAR, GATE = range(4)
    late = slice(C, TP)
    lnw, lnb, rk = vcol(k, 'ln_x_w'), vcol(k, 'ln_x_b'), vcol(k, 'r_k')
    prod_r, cent_r, sq_r, var_r, rs_r, bon_r, y_r, fin_r, sums, hid_in, hid_h, hid_l, gate_d = (
        k.sem("o_" + n) for n in ("prod", "cent", "sq", "var", "rs", "bonus", "y", "fin", "sums", "hid_in", "hid_hi",
                                  "hid_lo", "gate_done"))
    with ExitStack() as tmp, nc.Block() as block:
        hid = r.aa[0:G_HALF, 0:2, 0:T]
        hid_hi, hid_lo = (tmp.enter_context(nc.sbuf_tensor(f"ghid_{n}", [G_HALF, 2, T], F32R)) for n in ("hi", "lo"))

        @block.sync
        def _(sp):
            for j in range(2):
                load_unit(k, sp, j, g.src(0, j), g.kt)
            sp.dma_start(hid, g_hid).then_inc(hid_in.h, 16)
            gemm_sync(k, sp, g, nxt)

        @block.scalar
        def _(act):
            for j in range(2):
                act.wait_ge(k.raw_loaded[j].h, 16 * (b + 1))
                split_hi(k, j, g.kt)
            nc.scalar.preload_act_table_set("natural_log_exp_and_others")
            act.wait_ge(hid_in.h, 16)
            nc.scalar.activation(hid_hi[:], hid, ACT.Copy).then_inc(hid_h.h, 1)

            def high(m):
                act.wait_ge(fin_r.h, m + 1)
                nc.scalar.activation(k.x_hi[:, m, META:T], fin[m % 2], ACT.Copy).then_inc(k.xh_ready.h, 1)

            for m in range(KT):
                q = m % 2
                act.wait_ge(cent_r.h, m + 1)
                nc.scalar.activation(sq[q], cent[q], ACT.Square).then_inc(sq_r.h, 1)
                act.wait_ge(var_r.h, m + 1)
                if m >= 2:
                    act.wait_ge(y_r.h, 2 * (m - 2) + 1)
                nc.scalar.activation(rs[q], ps[q][:, VAR, :], ACT.Ln, scale=1.0 / HD, bias=k.eps[:, 2:3])\
                    .then_inc(rs_r.h, 1)
                act.wait_ge(rs_r.h, 2 * m + 1)
                nc.scalar.activation(rs[q], rs[q], ACT.Exp, scale=-0.5).then_inc(rs_r.h, 1)
                if m:
                    high(m - 1)
            high(KT - 1)
            for j in range(2):
                act.wait_ge(k.raw_loaded[j].h, 16 * (b + 2))
                act.wait_ge(k.unit_done[j].h, b + 1)
                split_hi(k, j, nxt.kt)

        @block.vector
        def _(dve):
            for j in range(2):
                dve.wait_ge(k.hi_ready[j].h, b + 1)
                split_lo(k, j, g.kt)
            dve.wait_ge(hid_h.h, 1)
            nc.vector.tensor_tensor(hid_lo[:], hid, hid_hi[:].bitcast(F32), ALU.subtract).then_inc(hid_l.h, 1)

            def product(m):
                nc.vector.scalar_tensor_tensor(prod[m % 2], r.rr[:, m, late], rk(m), r.kk_in[:, m, late], ALU.mult,
                                               ALU.mult).then_inc(prod_r.h, 1)

            def finish(m):
                q = m % 2
                dve.wait_ge(rs_r.h, 2 * m + 2)
                nc.vector.scalar_tensor_tensor(cent[q], cent[q], lnw(m), rs[q], ALU.mult, ALU.mult).then_inc(y_r.h, 1)
                dve.wait_ge(y_r.h, 2 * m + 1)
                nc.vector.scalar_tensor_tensor(cent[q], cent[q], lnb(m), bon[q], ALU.add, ALU.add).then_inc(y_r.h, 1)
                dve.wait_ge(y_r.h, 2 * m + 2)
                dve.wait_ge(gate_d.h, m + 1)
                if m >= 2:
                    dve.wait_ge(k.xl_ready.h, k.xl_ready.n + m - 1)
                nc.vector.tensor_tensor(fin[q], cent[q], ps[q][:, GATE, :], ALU.mult).then_inc(fin_r.h, 1)

            product(0)
            for m in range(KT):
                q = m % 2
                if m < KT - 1:
                    product(m + 1)
                dve.wait_ge(sums.h, m + 1)
                if m >= 2:
                    dve.wait_ge(fin_r.h, m - 1)
                nc.vector.scalar_tensor_tensor(cent[q], ps[q][:, MEAN, :], -1.0 / HD, y[:, m, late], ALU.mult,
                                               ALU.add).then_inc(cent_r.h, 1)
                nc.vector.tensor_tensor(bon[q], ps[q][:, BONUS, :], r.vv[:, m, late], ALU.mult).then_inc(bon_r.h, 1)
                if m:
                    finish(m - 1)
            finish(KT - 1)
            for j in range(2):
                dve.wait_ge(k.hi_ready[j].h, b + 2)
                split_lo(k, j, nxt.kt)

        @block.gpsimd
        def _(pool):
            for m in range(KT):
                pool.wait_ge(k.xh_ready.h, k.xh_ready.n + m + 1)
                nc.gpsimd.tensor_tensor(k.x_lo[:, m, META:T], fin[m % 2], k.x_hi[:, m, META:T].bitcast(F32),
                                        ALU.subtract).then_inc(k.xl_ready.h, 1)

        @block.tensor
        def _(pe):
            for j in range(2):
                pe.wait_ge(k.lo_ready[j].h, b + 1)
            pe.wait_ge(hid_l.h, 1)

            def head_sums(m):
                q = m % 2
                pe.wait_ge(prod_r.h, m + 1)
                if m >= 2:
                    pe.wait_ge(bon_r.h, m - 1)
                nc.tensor.matmul(ps[q][:, MEAN, :], r.heads[:], y[:, m, late], start=True, stop=True)
                nc.tensor.matmul(ps[q][:, BONUS, :], r.heads[:], prod[q], start=True, stop=True).then_inc(sums.h, 1)

            head_sums(0)
            for m in range(KT):
                q = m % 2
                if m < KT - 1:
                    head_sums(m + 1)
                if m >= 2:
                    pe.wait_ge(fin_r.h, m - 1)
                for j in range(2):
                    for n, (w, x) in enumerate(((k.w_hi, hid_hi), (k.w_hi, hid_lo), (k.w_lo, hid_hi))):
                        last = nc.tensor.matmul(ps[q][:, GATE, :], w[j][0:G_HALF, m, :], x[:, j, META:T],
                                                start=j == 0 and n == 0, stop=j == 1 and n == 2)
                last.then_inc(gate_d.h, 1)
                pe.wait_ge(sq_r.h, m + 1)
                nc.tensor.matmul(ps[q][:, VAR, :], r.heads[:], sq[q], start=True, stop=True).then_inc(var_r.h, 1)
            pe.wait_ge(gate_d.h, KT)
            pe.sem_inc(k.unit_done[0].h, 1)
            pe.wait_ge(fin_r.h, KT)
            pe.sem_inc(k.unit_done[1].h, 1)
            pe.sem_inc(k.psum_free[0].h, 1)
            pe.sem_inc(k.psum_free[1].h, 1)
    for c in (k.xh_ready, k.xl_ready):
        c.n += KT
    k.bodies += 1


def final_stage(k, out):
    nc = k.nc
    gain = vcol(k, 'final_norm')
    groups = SEQ // P
    with ExitStack() as tmp, nc.Block() as block:
        sq = tmp.enter_context(nc.sbuf_tensor("sq_final", [P, KT, T], F32))
        tok = tmp.enter_context(nc.sbuf_tensor("tok_out", [P, groups, D], F32))
        turned = k.sem("turned")
        copied = [k.sem(f"copied{half}") for half in range(2)]

        @block.scalar
        def _(act):
            norm_scalar(k, act, sq, split=False)
            for g in range(groups):
                act.wait_ge(turned.h, g + 1)
                nc.scalar.activation(tok[:, g, 0:D // 2], k.psg[:, g, :], ACT.Copy).then_inc(copied[0].h, 1)

        @block.vector
        def _(dve):
            norm_vector(k, dve, sq, lambda m: sq[:, ds(m, 1), :], gain)
            for g in range(groups):
                dve.wait_ge(turned.h, groups + g + 1)
                nc.vector.tensor_copy(tok[:, g, D // 2:D], k.psx[:, g, :]).then_inc(copied[1].h, 1)

        @block.tensor
        def _(pe):
            norm_tensor(k, pe, sq)
            for half, ps in enumerate((k.psg, k.psx)):
                pe.wait_ge(k.xn_ready.h, k.xn_ready.n + (half + 1) * KT // 2)
                for g in range(groups):
                    for q in range(KT // 2):
                        last = nc.tensor.transpose(ps[:, g, q * P:q * P + P],
                                                   sq[:, half * KT // 2 + q, META + g * P:META + g * P + P], k.ident[:])
                    last.then_inc(turned.h, 1)

        @block.sync
        def _(sp):
            view = out[0].rearrange("(g p) f -> g p f", p=P)
            for half in range(2):
                cols = slice(half * D // 2, (half + 1) * D // 2)
                for g in range(groups):
                    sp.wait_ge(copied[half].h, g + 1)
                    sp.dma_start(view[g][:, cols], tok[:, g, cols]).then_inc(k.stored.h, 16)
            sp.wait_ge(k.stored.h, k.stored.n + 16 * 2 * groups)



def kernel(**inputs):
    import numpy as np
    import concourse.bacc as bacc
    from concourse.bass_utils import run_bass_kernel_spmd

    nc = bacc.Bacc("TRN2", target_bir_lowering=False, num_devices=1, dynamic_dma_scratch_size=1024)
    arrays, d = {}, {}
    for name in INPUTS:
        a = np.ascontiguousarray(inputs[name])
        arrays[f"in_{name}_dram"] = a
        d[name] = nc.dram_tensor(f"in_{name}_dram", a.shape, mybir.dt.from_np(a.dtype), kind="ExternalInput").ap()
    out = nc.dram_tensor("out_0_dram", (1, SEQ, D), F32, kind="ExternalOutput").ap()
    build_program(nc, d, out)
    r = run_bass_kernel_spmd(nc, [arrays], core_ids=[0])
    return r.results[0]["out_0_dram"]
```
